# Optimizing a Trainium2 kernel written in Bass

```python
import jax, jax.numpy as jnp
from jax import lax
import numpy as np

D_MODEL = 1024
BATCH = 1
SEQ = 512
DEPTH = 1

N_MIXERS = 2
EPS = 1e-6

DSW_PATTERNS = ((128, 1), (512, 4), (2048, 16))
DSW_GROUPS = len(DSW_PATTERNS)
DSW_HEADS = 16
DSW_HEAD_DIM = D_MODEL // DSW_HEADS
DSW_IN_DIM = 3 * DSW_GROUPS * DSW_HEADS * DSW_HEAD_DIM

GLA_HEADS = 4
GLA_DK = D_MODEL // 2
GLA_DV = D_MODEL
GLA_HK = GLA_DK // GLA_HEADS
GLA_HV = GLA_DV // GLA_HEADS
GLA_GATE_RANK = 16
GLA_TAU = 16.0
GLA_CHUNK = 64
GLA_SPLITS = (GLA_DK, 2 * GLA_DK, 2 * GLA_DK + GLA_DV, 2 * GLA_DK + GLA_DV + GLA_GATE_RANK)
GLA_IN_DIM = 2 * GLA_DK + 2 * GLA_DV + GLA_GATE_RANK

FFN_DIM = 2816
CONV_WIDTH = 3

N_ATTN_LAYERS = (DEPTH + 1) // N_MIXERS
N_GLA_LAYERS = DEPTH // N_MIXERS

kernel_name = "hybrid_dilated_attn_gla_convffn_adaln"

def rms_norm(x, gain):
    xf = x.astype(jnp.float32)
    y = xf * lax.rsqrt(jnp.mean(xf * xf, axis=-1, keepdims=True) + EPS)
    return (y * gain.astype(jnp.float32)).astype(x.dtype)

def modulate(x, gain, shift, scale):
    return rms_norm(x, gain) * (1 + scale[:, None, :]) + shift[:, None, :]

def dilated_window_attention(q, k, v, window, dilation):
    B, S, H, E = q.shape
    n_keys = window // dilation
    L = S // dilation
    nb = -(-L // n_keys)
    L_pad = nb * n_keys

    def to_blocks(t):
        t = t.reshape(B, L, dilation, H, E).transpose(0, 2, 1, 3, 4)
        t = jnp.pad(t, ((0, 0), (0, 0), (0, L_pad - L), (0, 0), (0, 0)))
        return t.reshape(B, dilation, nb, n_keys, H, E)

    def with_prev(t):
        prev = jnp.pad(t, ((0, 0), (0, 0), (1, 0), (0, 0), (0, 0), (0, 0)))[:, :, :-1]
        return jnp.concatenate([prev, t], axis=3)

    qb = to_blocks(q)
    kb = with_prev(to_blocks(k))
    vb = with_prev(to_blocks(v))

    s = jnp.einsum('brnqhe,brnkhe->brnhqk', qb, kb,
                   preferred_element_type=jnp.float32) * (E ** -0.5)
    qi = jnp.arange(n_keys)[:, None] + n_keys
    kj = jnp.arange(2 * n_keys)[None, :]
    dist = qi - kj
    band = (dist >= 0) & (dist <= n_keys)
    not_first = (jnp.arange(nb) > 0)[:, None, None]
    valid = band[None] & (not_first | (kj >= n_keys)[None])
    s = jnp.where(valid[:, None], s, -jnp.inf)

    m = jnp.max(s, axis=-1, keepdims=True)
    p = jnp.exp(s - m)
    denom = jnp.sum(p, axis=-1, keepdims=True)
    o = jnp.einsum('brnhqk,brnkhe->brnqhe', p / denom, vb.astype(jnp.float32))
    lse = jnp.swapaxes((m + jnp.log(denom))[..., 0], 3, 4)

    def from_blocks(t):
        t = t.reshape((B, dilation, L_pad) + t.shape[4:])[:, :, :L]
        t = jnp.swapaxes(t, 1, 2)
        return t.reshape((B, S) + t.shape[3:])

    return from_blocks(o), from_blocks(lse)

def dilated_mixture_attention(h, w_in, w_out):
    B, S, _ = h.shape
    qkv = (h @ w_in).reshape(B, S, 3, DSW_GROUPS, DSW_HEADS, DSW_HEAD_DIM)
    outs, lses = [], []
    for g, (window, dilation) in enumerate(DSW_PATTERNS):
        o, lse = dilated_window_attention(qkv[:, :, 0, g], qkv[:, :, 1, g], qkv[:, :, 2, g],
                                          window, dilation)
        outs.append(o)
        lses.append(lse)
    weights = jax.nn.softmax(jnp.stack(lses, axis=0), axis=0)
    o = jnp.sum(weights[..., None] * jnp.stack(outs, axis=0), axis=0)
    return o.reshape(B, S, D_MODEL).astype(h.dtype) @ w_out

def gated_linear_attention(h, w_in, w_gate, b_gate, norm_gain, w_out):
    B, S, _ = h.shape
    f32 = jnp.float32
    q, k, v, g_low, r = jnp.split(h @ w_in, list(GLA_SPLITS), axis=-1)
    log_a = jax.nn.log_sigmoid((g_low @ w_gate + b_gate).astype(f32)) / GLA_TAU

    nc = S // GLA_CHUNK

    def chunks(t, hd):
        return t.astype(f32).reshape(B, nc, GLA_CHUNK, GLA_HEADS, hd)

    q = chunks(q, GLA_HK) * (GLA_HK ** -0.5)
    k = chunks(k, GLA_HK)
    v = chunks(v, GLA_HV)
    b = jnp.cumsum(chunks(log_a, GLA_HK), axis=2)
    b_last = b[:, :, -1:]
    q_dec = q * jnp.exp(b)
    k_dec = k * jnp.exp(-b)
    k_to_end = k * jnp.exp(b_last - b)

    causal = jnp.tril(jnp.ones((GLA_CHUNK, GLA_CHUNK), dtype=bool))
    att = jnp.where(causal, jnp.einsum('bnihk,bnjhk->bnhij', q_dec, k_dec), 0.0)
    o_intra = jnp.einsum('bnhij,bnjhv->bnihv', att, v)

    d_state = jnp.einsum('bnjhk,bnjhv->bnhkv', k_to_end, v)
    decay = jnp.exp(b_last[:, :, 0])

    def step(state, inp):
        dec, ds = inp
        return dec[..., None] * state + ds, state

    s0 = jnp.zeros((B, GLA_HEADS, GLA_HK, GLA_HV), f32)
    _, starts = lax.scan(step, s0, (jnp.moveaxis(decay, 1, 0), jnp.moveaxis(d_state, 1, 0)))
    starts = jnp.moveaxis(starts, 0, 1)
    o_inter = jnp.einsum('bnihk,bnhkv->bnihv', q_dec, starts)

    o = (o_intra + o_inter).reshape(B, S, GLA_HEADS, GLA_HV)
    o = rms_norm(o, norm_gain) * jax.nn.silu(r.astype(f32).reshape(B, S, GLA_HEADS, GLA_HV))
    return o.reshape(B, S, GLA_DV).astype(h.dtype) @ w_out

def conv_ffn(h, w_up, conv_w, conv_b, w_down):
    a, u = jnp.split(h @ w_up, 2, axis=-1)
    a = lax.conv_general_dilated(a, conv_w[:, None, :], window_strides=(1,),
                                 padding=[(CONV_WIDTH - 1, 0)],
                                 dimension_numbers=('NWC', 'WIO', 'NWC'),
                                 feature_group_count=FFN_DIM) + conv_b
    return (jax.nn.silu(a) * u) @ w_down

def setup_inputs(seed: int = 0) -> dict:
    key = jax.random.key(seed)
    ks = jax.random.split(key, 20)
    D, F = D_MODEL, FFN_DIM

    def nrm(k, shape, scale):
        return jax.random.normal(k, shape, jnp.float32) * scale

    return {
        "x": nrm(ks[0], (BATCH, SEQ, D), 1.0),
        "c": nrm(ks[1], (BATCH, D), 1.0),
        "w_ada": nrm(ks[2], (DEPTH, D, 6 * D), 0.5 * D ** -0.5),
        "b_ada": nrm(ks[3], (DEPTH, 6 * D), 0.01),
        "norm_mix": 1.0 + nrm(ks[4], (DEPTH, D), 0.01),
        "norm_ffn": 1.0 + nrm(ks[5], (DEPTH, D), 0.01),
        "attn_w_in": nrm(ks[6], (N_ATTN_LAYERS, D, DSW_IN_DIM), D ** -0.5),
        "attn_w_out": nrm(ks[7], (N_ATTN_LAYERS, D, D), D ** -0.5),
        "gla_w_in": nrm(ks[8], (N_GLA_LAYERS, D, GLA_IN_DIM), D ** -0.5),
        "gla_w_gate": nrm(ks[9], (N_GLA_LAYERS, GLA_GATE_RANK, GLA_DK), GLA_GATE_RANK ** -0.5),
        "gla_b_gate": nrm(ks[10], (N_GLA_LAYERS, GLA_DK), 0.01),
        "gla_norm": 1.0 + nrm(ks[11], (N_GLA_LAYERS, GLA_HV), 0.01),
        "gla_w_out": nrm(ks[12], (N_GLA_LAYERS, GLA_DV, D), GLA_DV ** -0.5),
        "ffn_w_up": nrm(ks[13], (DEPTH, D, 2 * F), D ** -0.5),
        "ffn_conv_w": nrm(ks[14], (DEPTH, CONV_WIDTH, F), CONV_WIDTH ** -0.5),
        "ffn_conv_b": nrm(ks[15], (DEPTH, F), 0.01),
        "ffn_w_down": nrm(ks[16], (DEPTH, F, D), F ** -0.5),
        "norm_final": 1.0 + nrm(ks[17], (D,), 0.01),
    }

def reference(x, c, w_ada, b_ada, norm_mix, norm_ffn, attn_w_in, attn_w_out,
              gla_w_in, gla_w_gate, gla_b_gate, gla_norm, gla_w_out,
              ffn_w_up, ffn_conv_w, ffn_conv_b, ffn_w_down, norm_final):
    cond = jax.nn.silu(c)
    for i in range(DEPTH):
        mod = cond @ w_ada[i] + b_ada[i]
        sh1, sc1, g1, sh2, sc2, g2 = jnp.split(mod, 6, axis=-1)
        h = modulate(x, norm_mix[i], sh1, sc1)
        j = i // N_MIXERS
        if i % N_MIXERS == 0:
            y = dilated_mixture_attention(h, attn_w_in[j], attn_w_out[j])
        else:
            y = gated_linear_attention(h, gla_w_in[j], gla_w_gate[j], gla_b_gate[j],
                                       gla_norm[j], gla_w_out[j])
        x = x + g1[:, None, :] * y
        h = modulate(x, norm_ffn[i], sh2, sc2)
        x = x + g2[:, None, :] * conv_ffn(h, ffn_w_up[i], ffn_conv_w[i], ffn_conv_b[i], ffn_w_down[i])
    return rms_norm(x, norm_final)


_drawn_inputs = setup_inputs


def setup_inputs(seed=0):
    import zlib

    import numpy as np

    out = dict(_drawn_inputs(seed))
    spreads = {}
    factors = {'b_ada': 6.331, 'norm_mix': 8.0, 'norm_ffn': 8.0, 'ffn_conv_b': 8.0, 'norm_final': 5.746}
    for name, (base, spread) in spreads.items():
        noise = np.random.default_rng([zlib.crc32(name.encode()), seed]).standard_normal(out[name].shape)
        drawn = base * np.exp(spread * noise) if base else spread * noise
        out[name] = __import__('jax').numpy.asarray(drawn.astype(out[name].dtype))
    for name, factor in factors.items():
        out[name] = (out[name] * factor).astype(out[name].dtype)
    return out
```

```python
from contextlib import ExitStack

import concourse.bass as bass
from concourse import mybir

F32 = mybir.dt.float32
F32R = mybir.dt.float32r
ACT = mybir.ActivationFunctionType
ALU = mybir.AluOpType

P = 128
T = 512
D = 1024
KT = D // P
NT = T // P
H, E = 16, 64
PAIRS = H // 2
GROUPS = 3
FF = 2816
FT = FF // P
HALF = T // 2
QUAD = 32
EPS = 1e-6
SCORE_SCALE = float(E) ** -0.5
MASKED = -3.0e38
MIX_STEPS = 8

STRIPS = 3 * GROUPS
RING = 3
QKV_STRIPS = PAIRS * STRIPS
OUT_STRIPS = KT
FRAW, FRING = 2, 4
UP_STRIPS = 2 * FT
PT_RING = 4
MOD = 6 * KT
MOD1 = 2 * KT
ROWS_A = MOD + 2 * KT
ROWS_B = 4 * FT


def strip_of(s):
    if s < GROUPS:
        return "v", s
    return "qk"[(s - GROUPS) % 2], (s - GROUPS) // 2


def in_order(group, which, src, dst):
    if which == "v" or (group == 0 and which == "k"):
        return src, dst
    if group == 0:
        return (src.rearrange("p (b j r) -> p b j r", b=NT, r=4),
                dst.rearrange("p (b r j) -> p b j r", b=NT, r=4))
    return src.rearrange("p (j r) -> p j r", r=4), dst.rearrange("p (r j) -> p j r", r=4)


def decoder_layer(nc, x, c, w_ada, b_ada, norm_mix, norm_ffn, attn_w_in, attn_w_out,
                  ffn_w_up, ffn_conv_w, ffn_conv_b, ffn_w_down, norm_final, out):
    x_rows = x[0].rearrange("(i p) d -> i p d", p=P)
    out_rows = out[0].rearrange("(i p) d -> i p d", p=P)
    c_cols = c[0].rearrange("(p t) -> p t", t=KT)
    ada = w_ada[0].rearrange("(p t) n -> p t n", t=KT)
    w_qkv = attn_w_in[0].rearrange("(t p) n -> p t n", p=P)
    w_o = attn_w_out[0].rearrange("(t p) n -> p t n", p=P)
    w_up = ffn_w_up[0].rearrange("(t p) n -> p t n", p=P)
    w_down = ffn_w_down[0].rearrange("(f p) n -> f p n", p=P)

    ctx = ExitStack()
    with ctx:
        def tensor(scope, name, shape, dt=F32):
            return scope.enter_context(nc.sbuf_tensor(name, shape, dt))

        def sem(name):
            return ctx.enter_context(nc.semaphore(name))

        xT = tensor(ctx, "xT", [P, KT, T])
        raw = tensor(ctx, "raw", [P, RING, KT, P])
        wh = tensor(ctx, "wh", [P, FRING, KT, P], F32R)
        wl = tensor(ctx, "wl", [P, FRING, KT, P], F32R)
        ident = tensor(ctx, "ident", [P, P])
        ones = tensor(ctx, "ones", [P, P])
        mask = tensor(ctx, "mask", [P, 2, HALF])
        cols_a = tensor(ctx, "cols_a", [P, ROWS_A])
        cols_b = tensor(ctx, "cols_b", [P, ROWS_B])
        mod_raw = tensor(ctx, "mod_raw", [P, MOD])
        mod = tensor(ctx, "mod", [P, MOD])
        gain = tensor(ctx, "gain", [P, 2, KT])
        cond = tensor(ctx, "cond", [P, 5, KT])
        stat = tensor(ctx, "stat", [P, 2, NT, 2, 2])
        swap = tensor(ctx, "swap", [P, 2, NT, 2, 2])
        nmax = tensor(ctx, "nmax", [P, 2, NT, 2])
        mix = tensor(ctx, "mix", [P, 9, 2, NT, 2])
        acc = tensor(ctx, "acc", [P, T])
        same = tensor(ctx, "same", [4, P])
        warm = tensor(ctx, "warm", [P, 2])
        rstd_o = tensor(ctx, "rstd_o", [P, 4, NT])
        ssq_o = tensor(ctx, "ssq_o", [P, NT, 2])

        scope_a = ExitStack()
        q_t = tensor(scope_a, "q_t", [P, 2, GROUPS, T])
        k_t = tensor(scope_a, "k_t", [P, 2, GROUPS, T])
        v_n = tensor(scope_a, "v_n", [P, 2, GROUPS, NT, P])
        v_t = tensor(scope_a, "v_t", [P, 2, T])
        probs = tensor(scope_a, "probs", [P, 2, 2, NT, HALF])
        p_t = tensor(scope_a, "p_t", [P, PT_RING, T])
        ada_raw = tensor(scope_a, "ada_raw", [P, KT // 2, T])
        o_a = tensor(scope_a, "o_a", [P, T])
        o_sum = tensor(scope_a, "o_sum", [P, T])
        oh = tensor(scope_a, "oh", [P, PAIRS, T], F32R)
        ol = tensor(scope_a, "ol", [P, PAIRS, T], F32R)
        hh = tensor(scope_a, "hh", [P, KT, T], F32R)
        hl = tensor(scope_a, "hl", [P, KT, T], F32R)
        scope_a.close()
        scope_s = ExitStack()
        ada1 = tensor(scope_s, "ada1", [P, 4, MOD1 * P])
        acc1 = tensor(scope_s, "acc1", [P, MOD1 * P])
        x_nat = tensor(scope_s, "x_nat", [P, NT, D])
        rows_a = tensor(scope_s, "rows_a", [ROWS_A, P])
        rows_b = tensor(scope_s, "rows_b", [ROWS_B, P])
        sq = tensor(scope_s, "sq", [P, 2, T])
        var = tensor(scope_s, "var", [P, T])
        rstd = tensor(scope_s, "rstd", [P, T])
        xn = tensor(scope_s, "xn", [P, 2, T])
        scope_s.close()
        scope_f = ExitStack()
        sq2 = tensor(scope_f, "sq2", [P, 2, T])
        sq_sum = tensor(scope_f, "sq_sum", [P, T])
        var2 = tensor(scope_f, "var2", [P, T])
        rstd2 = tensor(scope_f, "rstd2", [P, T])
        xn2 = tensor(scope_f, "xn2", [P, 2, T])
        fh = tensor(scope_f, "fh", [P, KT, T], F32R)
        fl = tensor(scope_f, "fl", [P, KT, T], F32R)
        act_h = tensor(scope_f, "act_h", [P, FT, T], F32R)
        act_l = tensor(scope_f, "act_l", [P, FT, T], F32R)
        gate_in = tensor(scope_f, "gate_in", [P, T])
        gate = tensor(scope_f, "gate", [P, T])
        scope_f.close()
        scope_e = ExitStack()
        out_n = tensor(scope_e, "out_n", [P, NT, D])
        nfin = tensor(scope_e, "nfin", [P, D])
        scope_e.close()

        banks = [ctx.enter_context(nc.psum_tensor(f"bank{i}", [P, T], F32)) for i in range(8)]
        proj, score, turn, o_acc = banks[0:2], banks[2:4], banks[4:6], banks[6:8]
        squares = banks[5]

        x_in, c_in, rows_in, nfin_in = sem("x_in"), sem("c_in"), sem("rows_in"), sem("nfin_in")
        ada1_in = [sem(f"ada1_in{i}") for i in range(4)]
        raw_in = [sem(f"raw_in{i}") for i in range(RING)]
        ada_in = sem("ada_in")
        const_done = sem("const_done")
        cond_step, mod_step = sem("cond_step"), sem("mod_step")
        acc1_step = sem("acc1_step")
        start_turned = sem("start_turned")
        start_taken = sem("start_taken")
        sq_done, sq_summed, sq_added = sem("sq_done"), sem("sq_summed"), sem("sq_added")
        norm_step, root_done = sem("norm_step"), sem("root_done")
        xn_done, xn_read = sem("xn_done"), sem("xn_read")
        hh_done, hl_done = sem("hh_done"), sem("hl_done")
        mod1_done, mod1_taken = sem("mod1_done"), sem("mod1_taken")
        same_done = sem("same_done")
        h_ready, l_ready = sem("h_ready"), sem("l_ready")
        strip_done, strip_taken = sem("strip_done"), sem("strip_taken")
        acc_step = sem("acc_step")
        y_done = sem("y_done")
        turned = [sem("turned0"), sem("turned1")]
        turn_taken = [sem("turn_taken0"), sem("turn_taken1")]
        scored, masked, nmax_done, exp_done = sem("scored"), sem("masked"), sem("nmax_done"), sem("exp_done")
        swapped, mix_dve, mix_act = sem("swapped"), sem("mix_dve"), sem("mix_act")
        scaled, pv_done = sem("scaled"), sem("pv_done")
        oa_copied, o_summed, oh_done, ol_done = sem("oa_copied"), sem("o_summed"), sem("oh_done"), sem("ol_done")
        x1_done = sem("x1_done")
        scores_seen, strip_seen = sem("scores_seen"), sem("strip_seen")
        fraw_in = [sem(f"fraw_in{i}") for i in range(FRAW)]
        fh_ready, fl_ready, fstrip_done = sem("fh_ready"), sem("fl_ready"), sem("fstrip_done")
        tap2_done, tap1_done, tap0_done = sem("tap2_done"), sem("tap1_done"), sem("tap0_done")
        gate_done, gated, act_h_done, act_l_done = sem("gate_done"), sem("gated"), sem("act_h_done"), sem("act_l_done")
        x2_done, nat_done, ssq_done, rstd_step, out_done, stored = (
            sem("x2_done"), sem("nat_done"), sem("ssq_done"), sem("rstd_step"), sem("out_done"), sem("stored"))

        block = ctx.enter_context(nc.Block())

        def turns_before(n):
            return 0 if isinstance(n, int) and n == 0 else 6 * n - 4

        SCORE_AT = {0: 0, 2: 1, 4: 2, 6: 3}
        TURN_V_AT = {3: 0, 5: 1, 7: 2}
        ADA_READ_AT = {0: 0, 1: 1, 2: 2, 3: 3, 5: 4, 6: 5, 7: 6, 8: 7}
        ADA_AT = 10
        TURN_P_AT = {12: 0, 14: 1, 15: 2, 16: 3}
        PV_AT = {14: 0, 15: 1, 16: 2, 17: 3}
        HALVES = 2 * STRIPS
        FILL_AT = {1: (0, 0), 3: (0, 1), 5: (1, 0), 7: (1, 1), 9: (2, 0), 10: (2, 1), 12: (3, 0), 17: (3, 1)}
        OUT_SPLIT_AT = {2: 2, 4: 3}
        OUT_AHEAD = 4
        out_banks = banks[0:OUT_AHEAD]

        def columns(eng, at, n):
            return slice(at, at + n) if isinstance(at, int) else bass.ds(at, n)

        def bodies(eng, body):
            body(0, 0, True, False)
            with eng.Fori(0, (PAIRS - 2) // 2) as m:
                body(2 * m + 1, 1, True, True)
                body(2 * m + 2, 0, True, True)
            body(PAIRS - 1, 1, True, True)
            body(PAIRS, 0, False, True)

        def p_blocks(j):
            tiles = (2 * (j % 2), 2 * (j % 2) + 1)
            return [(b, part) for b in tiles for part in range(2) if not (j == 0 and b == 0 and part == 0)]

        def tile_of(t, f):
            at = slice(f, f + 1) if isinstance(f, int) else bass.ds(f, 1)
            return t[:, at].rearrange("p a n -> p (a n)")

        def tap(k, f):
            return cols_b[:, FT * k + f:FT * k + f + 1] if isinstance(f, int) else cols_b[:, bass.ds(FT * k + f, 1)]

        def split_slot(split, j, u, value, ready, dst):
            slot = u % FRING
            if dst is wh:
                if isinstance(j, int) and j < FRING:
                    free = (strip_done, QKV_STRIPS + OUT_STRIPS - FRING + j + 1)
                else:
                    free = (fstrip_done, j - FRING + 1)
                split(fraw_in[u % FRAW], value, raw[:, u % FRAW], wh[:, slot], free, ready)
            else:
                split(fh_ready, j + 1, raw[:, u % FRAW], wh[:, slot], wl[:, slot], ready)

        def split_ffn(split, i, u, ready, dst):
            split_slot(split, 4 * i + u + 3, (u + 3) % FRING, 16 * (2 * i + (u + 3) // 2 + 1), ready, dst)

        def split_down(split, k, u, pair, ready, dst):
            split_slot(split, UP_STRIPS + k + 3, (u + 3) % FRING, 16 * (UP_STRIPS // 2 + pair + 2 + u % 2), ready, dst)

        def split_out(split, o, ready, dst):
            g = QKV_STRIPS + o
            if dst is wh:
                free = None if o == FRING - 1 else (strip_done, g - RING + 1 if o < FRING else g - FRING + 1)
                split(raw_in[g % RING], 16 * (g // RING + 1), raw[:, g % RING], wh[:, o % FRING], free, ready)
            else:
                split(h_ready, g + 1, raw[:, g % RING], wh[:, o % FRING], wl[:, o % FRING], ready)

        def split_ahead(split, o, ready, f_ready, dst):
            if o + FRING < OUT_STRIPS:
                split_out(split, o + FRING, ready, dst)
            elif o + FRING - OUT_STRIPS < 3:
                j = o + FRING - OUT_STRIPS
                split_slot(split, j, j, 16 * (j // 2 + 1), f_ready, dst)

        def downs(eng, down):
            down(0, 0, 0)
            down(1, 1, 0)
            with eng.Fori(0, (FT - 6) // 4) as m:
                for u in range(4):
                    down(4 * m + 2 + u, (2 + u) % FRING, 2 * m + 1 + u // 2)
            for k in range(FT - 4, FT):
                down(k, k % FRING, k // 2)

        @block.sync
        def _(sp):
            sp.dma_start(cond[:, 0, :], c_cols).then_inc(c_in, 16)
            for i in range(NT):
                sp.dma_start(x_nat[:, i, :], x_rows[i]).then_inc(x_in, 16)
            sp.dma_start(rows_a[0:MOD], b_ada[0].rearrange("(r p) -> r p", p=P)).then_inc(rows_in, 16)
            sp.dma_start(rows_a[MOD:MOD + KT], norm_mix[0].rearrange("(r p) -> r p", p=P)).then_inc(rows_in, 16)
            sp.dma_start(rows_a[MOD + KT:ROWS_A], norm_ffn[0].rearrange("(r p) -> r p", p=P)).then_inc(rows_in, 16)
            sp.dma_start(rows_b[0:3 * FT], ffn_conv_w[0].rearrange("k (r p) -> (k r) p", p=P)).then_inc(rows_in, 16)
            sp.dma_start(rows_b[3 * FT:ROWS_B], ffn_conv_b[0].rearrange("(r p) -> r p", p=P)).then_inc(rows_in, 16)
            for t in range(KT):
                if t >= 4:
                    sp.wait_ge(acc1_step, t - 3)
                sp.dma_start(ada1[:, t % 4, :], ada[:, t, 0:MOD1 * P]).then_inc(ada1_in[t % 4], 16)

            def load_strips(n, first):
                for s in range(STRIPS):
                    kind, g = strip_of(s)
                    at = {"q": 0, "k": 1, "v": 2}[kind] * GROUPS * D + g * D
                    src = w_qkv[:, :, columns(sp, at + P * n, P)]
                    if s in (2, 5):
                        half = 0 if s == 2 else 1
                        src_ada = ada[:, half * KT // 2:(half + 1) * KT // 2, columns(sp, MOD1 * P + T * n, T)]
                    if not (first and s < RING):
                        sp.wait_ge(h_ready, STRIPS * n + s - RING + 1)
                        sp.wait_ge(l_ready, STRIPS * n + s - RING + 1)
                        if at == 0:
                            sp.sem_inc(strip_seen, 1)
                    sp.dma_start(raw[:, s % RING], src).then_inc(raw_in[s % RING], 16)
                    if s in (2, 5):
                        if not (first and half == 0):
                            sp.wait_ge(acc_step, KT * n + 4 * half)
                        elif first:
                            sp.wait_ge(hl_done, KT)
                        sp.dma_start(ada_raw[:], src_ada).then_inc(ada_in, 16)
            load_strips(0, True)
            with sp.Fori(1, PAIRS) as n:
                load_strips(n, False)
            for o in range(OUT_STRIPS):
                g = QKV_STRIPS + o
                sp.wait_ge(h_ready, g - RING + 1)
                sp.wait_ge(l_ready, g - RING + 1)
                sp.dma_start(raw[:, g % RING], w_o[:, :, P * o:P * (o + 1)]).then_inc(raw_in[g % RING], 16)

            def up_columns(f, u):
                return w_up[:, :, columns(sp, FF * u + P * f, P)]
            for j in range(FRAW):
                sp.wait_ge(h_ready, QKV_STRIPS + OUT_STRIPS - 1 + j)
                sp.wait_ge(l_ready, QKV_STRIPS + OUT_STRIPS - 1 + j)
                sp.dma_start(raw[:, j], up_columns(0, j)).then_inc(fraw_in[j], 16)
            with sp.Fori(1, FT) as f:
                for u in range(2):
                    src = up_columns(f, u)
                    sp.wait_ge(fh_ready, 2 * f + u - FRAW + 1)
                    sp.wait_ge(fl_ready, 2 * f + u - FRAW + 1)
                    sp.dma_start(raw[:, u], src).then_inc(fraw_in[u], 16)
            with sp.Fori(0, FT // 2) as m:
                for u in range(2):
                    j = UP_STRIPS + 2 * m + u
                    src = w_down[columns(sp, 2 * m + u, 1)].rearrange("a p n -> p (a n)")
                    sp.wait_ge(fh_ready, j - FRAW + 1)
                    sp.wait_ge(fl_ready, j - FRAW + 1)
                    sp.dma_start(raw[:, u].rearrange("p t n -> p (t n)"), src).then_inc(fraw_in[u], 16)
            sp.wait_ge(act_l_done, FT)
            sp.wait_ge(fstrip_done, UP_STRIPS)
            sp.dma_start(nfin[:], norm_final.partition_broadcast(P)).then_inc(nfin_in, 16)
            for i in range(NT):
                sp.wait_ge(out_done, 2 * (i + 1))
                sp.dma_start(out_rows[i], out_n[:, i, :]).then_inc(stored, 16)
            sp.wait_ge(stored, 16 * NT)

        @block.gpsimd
        def _(pool):
            nc.gpsimd.memset(ident[:], 0.0).then_inc(const_done, 1)
            nc.gpsimd.memset(ones[:], 1.0).then_inc(const_done, 1)
            nc.gpsimd.memset(mask[:], 0.0).then_inc(const_done, 1)
            nc.gpsimd.memset(same[:], 0.0).then_inc(const_done, 1)
            pool.wait_ge(const_done, 4)
            nc.gpsimd.affine_select(out=ident[:], in_=ident[:], compare_op=ALU.not_equal, fill=1.0, base=0,
                                    pattern=[[-1, P]], channel_multiplier=1).then_inc(const_done, 1)
            view = same[:].rearrange("p (a i) -> p a i", i=4)
            nc.gpsimd.affine_select(out=view, in_=view, compare_op=ALU.not_equal, fill=1.0, base=0,
                                    pattern=[[0, P // 4], [-1, 4]], channel_multiplier=1).then_inc(const_done, 1)
            pool.wait_ge(const_done, 6)
            for r in range(4):
                if r:
                    pool.wait_ge(const_done, 6 + 2 * r)
                part = mask[QUAD * r:QUAD * (r + 1), 0]
                nc.gpsimd.affine_select(out=part[:, 0:P], in_=part[:, 0:P], compare_op=ALU.is_ge, fill=MASKED,
                                        base=-r, pattern=[[1, P]], channel_multiplier=-4).then_inc(const_done, 1)
                nc.gpsimd.affine_select(out=part[:, P:HALF], in_=part[:, P:HALF], compare_op=ALU.is_ge, fill=MASKED,
                                        base=r, pattern=[[-1, P]], channel_multiplier=4).then_inc(const_done, 1)
            pool.wait_ge(const_done, 14)
            for g in range(2):
                part = mask[:, 1, P * g:P * (g + 1)]
                nc.gpsimd.affine_select(out=part, in_=part, compare_op=ALU.is_ge, fill=MASKED,
                                        base=0, pattern=[[-1, P]], channel_multiplier=1).then_inc(const_done, 1)

        @block.tensor
        def _(pe):
            pe.wait_ge(const_done, 16)
            pe.wait_ge(x_in, 16 * NT)
            for t in range(KT):
                if t >= 4:
                    pe.wait_ge(start_taken, t - 3)
                for i in range(NT):
                    last = nc.tensor.transpose(banks[t % 4][:, P * i:P * (i + 1)], x_nat[:, i, P * t:P * (t + 1)], ident[:])
                last.then_inc(start_turned, 1)
            pe.wait_ge(rows_in, 5 * 16)
            nc.tensor.transpose(banks[4][:, 0:ROWS_A], rows_a[:], ident[0:ROWS_A, 0:ROWS_A])
            nc.tensor.transpose(banks[4][:, P:P + ROWS_B], rows_b[:], ident[0:ROWS_B, 0:ROWS_B]).then_inc(start_turned, 1)
            nc.tensor.matmul(banks[7][:, 0:P], same[:], same[:], start=True, stop=True).then_inc(same_done, 1)

            for t in range(KT):
                pe.wait_ge(sq_done, t + 1)
                nc.tensor.matmul(squares[:], ones[:], sq[:, t % 2], start=(t == 0), stop=(t == KT - 1)
                                 ).then_inc(sq_summed, 1)
            pe.wait_ge(acc1_step, KT)
            for j in range(MOD1):
                last = nc.tensor.matmul(banks[6][:, j:j + 1], acc1[:, P * j:P * (j + 1)], ones[:, 0:1],
                                        start=True, stop=True)
            last.then_inc(mod1_done, 1)

            def half_strip(bank, slot, half, xh, xl, first=False):
                for t in range(half * KT // 2, (half + 1) * KT // 2):
                    if first:
                        pe.wait_ge(hl_done, t + 1)
                    nc.tensor.matmul(bank[:], wl[:, slot, t], xh[:, t], start=(t == 0), stop=False)
                    nc.tensor.matmul(bank[:], wh[:, slot, t], xh[:, t], start=False, stop=False)
                    last = nc.tensor.matmul(bank[:], wh[:, slot, t], xl[:, t], start=False, stop=(t == KT - 1))
                return last

            def make_scores(n, par, d):
                if d == 0:
                    pe.wait_ge(strip_taken, STRIPS * n)
                pe.wait_ge(masked, 4 * (n - 1) + d + 1)
                side, tiles = d // 2, (2 * (d % 2), 2 * (d % 2) + 1)
                for b in tiles:
                    at = HALF * (b % 2)
                    if side == 0:
                        lo = P * max(b - 1, 0)
                        for hd in range(2):
                            e = slice(E * hd, E * (hd + 1))
                            last = nc.tensor.matmul(score[hd][:, at + (P if b == 0 else 0):at + HALF],
                                                    q_t[e, par, 0, P * b:P * (b + 1)],
                                                    k_t[e, par, 0, lo:P * (b + 1)], start=True, stop=True)
                    else:
                        for g in (1, 2):
                            for hd in range(2):
                                e = slice(E * hd, E * (hd + 1))
                                last = nc.tensor.matmul(score[hd][:, at + P * (g - 1):at + P * g],
                                                        q_t[e, par, g, P * b:P * (b + 1)],
                                                        k_t[e, par, g, P * b:P * (b + 1)], start=True, stop=True)
                last.then_inc(scored, 1)

            def turn_values(n, par, g):
                k, use = g % 2, g // 2
                pe.wait_ge(strip_taken, STRIPS * n + g + 1)
                if not (isinstance(n, int) and n == 0 and use == 0):
                    pe.wait_ge(turn_taken[k], turns_before(n) + use)
                src = v_t[:, (par + g) % 2]
                for b in range(NT):
                    keys = src[:, P * b:P * (b + 1)] if g == 0 else src[:, b:T:4]
                    last = nc.tensor.transpose(turn[k][:, P * b:P * (b + 1)], keys, ident[:])
                last.then_inc(turned[k], 1)

            def sum_ada(n):
                pe.wait_ge(acc_step, KT * (n + 1))
                pe.wait_ge(turn_taken[1], turns_before(n) + 1)
                for j in range(NT):
                    last = nc.tensor.matmul(turn[1][:, j:j + 1], acc[:, P * j:P * (j + 1)], ones[:, 0:1],
                                            start=True, stop=True)
                last.then_inc(turned[1], 1)

            def turn_probs(n, u, before):
                hd, j, k = u % 2, u // 2, u % 2
                pe.wait_ge(scaled, 8 * (n - 1) + u + 1)
                pe.wait_ge(turn_taken[k], turns_before(n) + before + j)
                for i, (b, part) in enumerate(p_blocks(j)):
                    last = nc.tensor.transpose(turn[k][:, P * i:P * (i + 1)],
                                               probs[:, hd, j // 2, b, P * part:P * (part + 1)], ident[:])
                last.then_inc(turned[k], 1)

            def weigh_values(n, par, u, before):
                hd, j, k = u % 2, u // 2, u % 2
                e = slice(E * hd, E * (hd + 1))
                pe.wait_ge(turn_taken[k], turns_before(n) + before + j + 1)
                if u == 0:
                    pe.wait_ge(o_summed, n)
                side = j // 2
                blocks = p_blocks(j)
                for i, (b, part) in enumerate(blocks):
                    if side == 0:
                        values = v_n[:, par, 0, b - 1 + part, e]
                    else:
                        values = v_n[:, par, 1 + part, b, e]
                    first = i == 0 or blocks[i - 1][0] != b
                    final = i == len(blocks) - 1 or blocks[i + 1][0] != b
                    last = nc.tensor.matmul(o_acc[side][e, P * b:P * (b + 1)], values, p_t[:, u % PT_RING, P * i:P * (i + 1)],
                                            start=first, stop=final)
                last.then_inc(pv_done, 1)

            def out_tiles(o, tiles):
                for t in tiles:
                    nc.tensor.matmul(out_banks[o % 4][:], wl[:, o % FRING, t], oh[:, t], start=(t == 0), stop=False)
                    nc.tensor.matmul(out_banks[o % 4][:], wh[:, o % FRING, t], oh[:, t], start=False, stop=False)
                    last = nc.tensor.matmul(out_banks[o % 4][:], wh[:, o % FRING, t], ol[:, t], start=False,
                                            stop=(t == KT - 1))
                return last

            def begin_out(o, part):
                if part == 0:
                    pe.wait_ge(l_ready, QKV_STRIPS + o + 1)
                    if o < 2:
                        pe.wait_ge(strip_taken, QKV_STRIPS - 1 + o)
                        pe.wait_ge(ol_done, KT // 2)
                    else:
                        pe.wait_ge(masked, 4 * PAIRS + 1)
                    out_tiles(o, range(KT // 2))
                else:
                    pe.wait_ge(ol_done, PAIRS - 1)
                    out_tiles(o, range(KT // 2, KT - 1))

            def body(n, par, project, attend):
                before = 2 if project else 0
                for h in range(HALVES):
                    s = h // 2
                    if project:
                        g = STRIPS * n + s
                        if h % 2 == 0:
                            pe.wait_ge(l_ready, g + 1)
                            if not isinstance(g, int) or g >= 2:
                                pe.wait_ge(strip_taken, g - 1)
                        last = half_strip(proj[(par + s) % 2], s % RING, h % 2, hh, hl,
                                          first=isinstance(g, int) and g == 0)
                        if h % 2 == 1:
                            last.then_inc(strip_done, 1)
                        if h in TURN_V_AT:
                            turn_values(n, par, TURN_V_AT[h])
                        if h == ADA_AT:
                            sum_ada(n)
                    if attend:
                        if h in SCORE_AT:
                            make_scores(n, 1 - par, SCORE_AT[h])
                        if h in PV_AT:
                            for u in (2 * PV_AT[h], 2 * PV_AT[h] + 1):
                                weigh_values(n, 1 - par, u, before)
                        if h in TURN_P_AT:
                            for u in (2 * TURN_P_AT[h], 2 * TURN_P_AT[h] + 1):
                                turn_probs(n, u, before)
                    if attend and not project and h in FILL_AT:
                        begin_out(*FILL_AT[h])
            bodies(pe, body)

            pe.wait_ge(ol_done, PAIRS)
            for o in range(OUT_STRIPS):
                if o >= OUT_AHEAD:
                    pe.wait_ge(l_ready, QKV_STRIPS + o + 1)
                    pe.wait_ge(x1_done, o - OUT_AHEAD + 1)
                out_tiles(o, range(KT - 1 if o < OUT_AHEAD else 0, KT)).then_inc(strip_done, 1)
            pe.wait_ge(sq_added, KT - 2)
            nc.tensor.matmul(squares[:], ones[:], sq_sum[:], start=True, stop=False)
            pe.wait_ge(sq_done, 2 * KT)
            nc.tensor.matmul(squares[:], ones[:], sq2[:, (KT - 1) % 2], start=False, stop=True).then_inc(sq_summed, 1)

            pe.wait_ge(fl_ready, 2)
            for t in range(KT):
                pe.wait_ge(hl_done, KT + t + 1)
                for j in range(2):
                    nc.tensor.matmul(banks[j][:], wl[:, j, t], fh[:, t], start=(t == 0), stop=False)
                    nc.tensor.matmul(banks[j][:], wh[:, j, t], fh[:, t], start=False, stop=False)
                    last = nc.tensor.matmul(banks[j][:], wh[:, j, t], fl[:, t], start=False, stop=(t == KT - 1))
                    if t == KT - 1:
                        last.then_inc(fstrip_done, 1)

            def up(i):
                for w in range(2):
                    for u in range(2):
                        j = 4 * i + 2 * w + u
                        f = 2 * i + w
                        if isinstance(j, int) and j < 2:
                            continue
                        pe.wait_ge(fl_ready, j + 1)
                        if u == 0 and not (isinstance(i, int) and i == 0):
                            pe.wait_ge(gated, f - 1)
                        bank, slot = banks[2 * w + u], 2 * w + u
                        for t in range(KT):
                            nc.tensor.matmul(bank[:], wl[:, slot, t], fh[:, t], start=(t == 0), stop=False)
                            nc.tensor.matmul(bank[:], wh[:, slot, t], fh[:, t], start=False, stop=False)
                            last = nc.tensor.matmul(bank[:], wh[:, slot, t], fl[:, t], start=False, stop=(t == KT - 1))
                        last.then_inc(fstrip_done, 1)
            up(0)
            with pe.Fori(1, FT // 2) as i:
                up(i)

            def down(k, u, pair):
                static = isinstance(k, int)
                final, slot = static and k == FT - 1, u
                pe.wait_ge(fl_ready, UP_STRIPS + k + 1)
                pe.wait_ge(act_l_done, k + 1)
                for o in range(KT):
                    if static and k == 0 and o in (4, 6):
                        pe.wait_ge(gated, FT - 1 + (o == 6))
                    start, stop = static and k == 0, final
                    at = slice(k, k + 1) if static else bass.ds(k, 1)
                    xh = act_h[:, at].rearrange("p a n -> p (a n)")
                    xl = act_l[:, at].rearrange("p a n -> p (a n)")
                    y = banks[(o + 4) % 8]
                    nc.tensor.matmul(y[:], wl[:, slot, o], xh, start=start, stop=False)
                    nc.tensor.matmul(y[:], wh[:, slot, o], xh, start=False, stop=False)
                    last = nc.tensor.matmul(y[:], wh[:, slot, o], xl, start=False, stop=stop)
                    if final:
                        last.then_inc(y_done, 1)
                if not final:
                    last.then_inc(fstrip_done, 1)
            downs(pe, down)

            for hf in range(2):
                pe.wait_ge(x2_done, KT // 2 * (hf + 1))
                for i in range(NT):
                    for o in range(4):
                        last = nc.tensor.transpose(banks[4 * (1 - hf) + i][:, P * o:P * (o + 1)],
                                                   xT[:, 4 * hf + o, P * i:P * (i + 1)], ident[:])
                    last.then_inc(nat_done, 1)

        @block.scalar
        def _(act):
            act.wait_ge(c_in, 16)
            nc.scalar.activation(cond[:, 1], cond[:, 0], ACT.Exp, scale=-1.0).then_inc(cond_step, 1)

            for t in range(KT):
                act.wait_ge(start_turned, t + 1)
                nc.scalar.activation(xT[:, t], banks[t % 4][:], ACT.Copy).then_inc(start_taken, 1)
            for t in range(KT):
                act.wait_ge(start_taken, t + 1)
                if t >= 2:
                    act.wait_ge(sq_summed, t - 1)
                nc.scalar.activation(sq[:, t % 2], xT[:, t], ACT.Square).then_inc(sq_done, 1)
            act.wait_ge(start_turned, KT + 1)
            nc.scalar.activation(cols_a[:], banks[4][:, 0:ROWS_A], ACT.Copy).then_inc(start_taken, 1)
            nc.scalar.activation(cols_b[:], banks[4][:, P:P + ROWS_B], ACT.Copy).then_inc(start_taken, 1)

            def root(q, v, r):
                act.wait_ge(norm_step, 2 * q + 1)
                nc.scalar.activation(r[:], v[:], ACT.Sqrt).then_inc(root_done, 1)
            root(0, var, rstd)

            def split_h(sem_in, value, src, dst, free, done):
                act.wait_ge(sem_in, value)
                if free is not None:
                    act.wait_ge(*free)
                nc.scalar.activation(dst, src, ACT.Copy).then_inc(done, 1)

            def split_qkv(n, s):
                g = STRIPS * n + s
                free = None if isinstance(g, int) and g < RING else (strip_done, g - RING + 1)
                split_h(raw_in[s % RING], 16 * (GROUPS * n + s // RING + 1), raw[:, s % RING], wh[:, s % RING],
                        free, h_ready)
            act.wait_ge(mod1_done, 1)
            nc.scalar.activation(mod_raw[:, 0:MOD1], banks[6][:, 0:MOD1], ACT.Copy).then_inc(mod1_taken, 1)
            split_qkv(0, 0)

            def high_part(q, x_norm, dst, shift):
                for t in range(KT):
                    act.wait_ge(xn_done, KT * q + t + 1)
                    nc.scalar.activation(dst[:, t], x_norm[:, t % 2], ACT.Identity,
                                         bias=mod[:, shift + t:shift + t + 1]).then_inc(hh_done, 1)
            high_part(0, xn, hh, 0)
            split_qkv(0, 1)

            def take_turn(n, use, dst, j=None):
                act.wait_ge(turned[1], turns_before(n) + use + 1)
                src = turn[1][:] if j is None else turn[1][:, 0:j]
                nc.scalar.activation(dst, src, ACT.Copy).then_inc(turn_taken[1], 1)

            def body(n, par, project, attend):
                before = 2 if project else 0
                for h in range(HALVES):
                    s = h // 2
                    if project:
                        if h % 2 == 0:
                            split_qkv(n, s + 2)
                        else:
                            act.wait_ge(strip_done, STRIPS * n + s + 1)
                            kind, g = strip_of(s)
                            dst = {"v": v_t[:, (par + g) % 2], "q": q_t[:, par, g], "k": k_t[:, par, g]}[kind]
                            src, dst = in_order(g, kind, proj[(par + s) % 2][:], dst)
                            nc.scalar.activation(dst, src, ACT.Copy).then_inc(strip_taken, 1)
                        if TURN_V_AT.get(h) == 1:
                            take_turn(n, 0, v_n[:, par, 1].rearrange("p b e -> p (b e)"))
                        if h == ADA_AT:
                            take_turn(n, 1, mod_raw[:, bass.ds(MOD1 + NT * n, NT)], NT)
                    if attend:
                        if h in SCORE_AT:
                            d = SCORE_AT[h]
                            act.wait_ge(nmax_done, 4 * (n - 1) + d + 1)
                            side = d // 2
                            for b in (2 * (d % 2), 2 * (d % 2) + 1):
                                for hd in range(2):
                                    tile = probs[:, hd, side, b, (P if d == 0 and b == 0 else 0):HALF]
                                    last = nc.scalar.activation(tile, tile, ACT.Exp, bias=nmax[:, side, b, hd:hd + 1],
                                                                scale=SCORE_SCALE, accum_out=stat[:, side, b, 1, hd:hd + 1])
                            last.then_inc(exp_done, 1)
                        if h == 8:
                            act.wait_ge(mix_dve, MIX_STEPS * (n - 1) + 3)
                            nc.scalar.activation(mix[:, 3:5], mix[:, 1:3], ACT.Exp, scale=SCORE_SCALE).then_inc(mix_act, 1)
                        if h in TURN_P_AT:
                            u = 2 * TURN_P_AT[h] + 1
                            take_turn(n, before + u // 2, p_t[:, u % PT_RING])
                    if attend and not project and h in OUT_SPLIT_AT:
                        split_out(split_h, OUT_SPLIT_AT[h], h_ready, wh)
                if attend:
                    act.wait_ge(pv_done, 8 * n)
                    nc.scalar.activation(o_a[:].rearrange("p (b j r) -> p b j r", b=NT, r=4),
                                         o_acc[0][:].rearrange("p (b r j) -> p b j r", b=NT, r=4),
                                         ACT.Copy).then_inc(oa_copied, 1)
                    act.wait_ge(o_summed, n + 1)
                    nc.scalar.activation(oh[:, bass.ds(n - 1, 1)].rearrange("p a n -> p (a n)"), o_sum[:],
                                         ACT.Copy).then_inc(oh_done, 1)
            bodies(act, body)

            nc.scalar.activation(warm[:, 0:1], ones[:, 0:1], ACT.Sqrt)
            for o in range(OUT_STRIPS):
                split_ahead(split_h, o, h_ready, fh_ready, wh)
                act.wait_ge(x1_done, o + 1)
                if o >= 3:
                    act.wait_ge(sq_added, o - 2)
                nc.scalar.activation(sq2[:, o % 2] if o else sq_sum[:], xT[:, o], ACT.Square).then_inc(sq_done, 1)
            root(1, var2, rstd2)
            high_part(1, xn2, fh, 3 * KT)

            def gate_branch(f):
                act.wait_ge(tap0_done, f + 1)
                if not (isinstance(f, int) and f == 0):
                    act.wait_ge(act_l_done, f)
                nc.scalar.activation(gate[:], gate_in[:], ACT.Silu).then_inc(gate_done, 1)
                act.wait_ge(gated, f + 1)
                nc.scalar.activation(tile_of(act_h, f), gate[:], ACT.Copy).then_inc(act_h_done, 1)

            def up(i):
                for w in range(2):
                    f = 2 * i + w
                    for u in range(2):
                        j = 4 * i + 2 * w + u
                        split_ffn(split_h, i, 2 * w + u, fh_ready, wh)
                        if u == 0 and not (isinstance(f, int) and f == 0):
                            gate_branch(f - 1)
                        if u == 1:
                            act.wait_ge(fstrip_done, j)
                            nc.scalar.activation(gate_in[:], banks[2 * w][:], ACT.Identity, bias=tap(3, f),
                                                 scale=tap(2, f)).then_inc(tap2_done, 1)
            up(0)
            with act.Fori(1, FT // 2) as i:
                up(i)
            gate_branch(FT - 1)

            def down(k, u, pair):
                if not (isinstance(k, int) and k >= FT - 3):
                    split_down(split_h, k, u, pair, fh_ready, wh)
            downs(act, down)

            nc.scalar.activation(warm[:, 1:2], ones[:, 0:1], ACT.Sqrt)
            for hf in range(2):
                for i in range(NT):
                    act.wait_ge(nat_done, NT * hf + i + 1)
                    nc.scalar.activation(out_n[:, i, T * hf:T * (hf + 1)], banks[4 * (1 - hf) + i][:], ACT.Square,
                                         accum_out=ssq_o[:, i, hf:hf + 1]).then_inc(ssq_done, 1)
            act.wait_ge(rstd_step, 2)
            nc.scalar.activation(rstd_o[:, 2], rstd_o[:, 1], ACT.Sqrt).then_inc(rstd_step, 1)

        @block.vector
        def _(dve):
            dve.wait_ge(cond_step, 1)
            nc.vector.tensor_scalar(cond[:, 2], cond[:, 1], 1.0, None, ALU.add).then_inc(cond_step, 1)
            dve.wait_ge(cond_step, 2)
            nc.vector.reciprocal(cond[:, 3], cond[:, 2]).then_inc(cond_step, 1)
            dve.wait_ge(cond_step, 3)
            nc.vector.tensor_tensor(cond[:, 4], cond[:, 0], cond[:, 3], ALU.mult).then_inc(cond_step, 1)
            dve.wait_ge(cond_step, 4)
            for t in range(KT):
                dve.wait_ge(ada1_in[t % 4], 16 * (t // 4 + 1))
                if t == 0:
                    nc.vector.tensor_scalar(acc1[:], ada1[:, 0], cond[:, 4, 0:1], None, ALU.mult).then_inc(acc1_step, 1)
                else:
                    dve.wait_ge(acc1_step, t)
                    nc.vector.scalar_tensor_tensor(acc1[:], ada1[:, t % 4], cond[:, 4, t:t + 1], acc1[:],
                                                   ALU.mult, ALU.add).then_inc(acc1_step, 1)

            def add_square(t):
                dve.wait_ge(sq_done, KT + t + 1)
                if t >= 2:
                    dve.wait_ge(sq_added, t - 1)
                nc.vector.tensor_tensor(sq_sum[:], sq_sum[:], sq2[:, t % 2], ALU.add).then_inc(sq_added, 1)

            def inverse_root(q, v, r):
                dve.wait_ge(sq_summed, KT + q)
                nc.vector.tensor_scalar(v[:], squares[:], 1.0 / D, EPS, ALU.mult, ALU.add).then_inc(norm_step, 1)
                dve.wait_ge(root_done, q + 1)
                nc.vector.reciprocal(r[:], r[:]).then_inc(norm_step, 1)
                dve.wait_ge(norm_step, 2 * q + 2)

            def modulation(lo, hi):
                nc.vector.tensor_tensor(mod[:, lo:hi], mod_raw[:, lo:hi], cols_a[:, lo:hi], ALU.add).then_inc(mod_step, 1)

            def gains(q, scale):
                nc.vector.scalar_tensor_tensor(gain[:, q], mod[:, scale:scale + KT], 1.0,
                                               cols_a[:, MOD + KT * q:MOD + KT * (q + 1)],
                                               ALU.add, ALU.mult).then_inc(mod_step, 1)

            dve.wait_ge(same_done, 1)
            dve.wait_ge(const_done, 16)
            nc.vector.tensor_scalar(xn[:, 0, 0:P], banks[7][:, 0:P], 1.0, -MASKED, ALU.subtract, ALU.mult
                                    ).then_inc(same_done, 1)
            dve.wait_ge(same_done, 2)
            nc.vector.tensor_tensor(mask[:, 1, P:HALF], mask[:, 1, P:HALF], xn[:, 0, 0:P], ALU.min).then_inc(same_done, 1)
            dve.wait_ge(same_done, 3)

            inverse_root(0, var, rstd)
            dve.wait_ge(mod1_taken, 1)
            dve.wait_ge(start_taken, KT + 2)
            modulation(0, MOD1)
            dve.wait_ge(mod_step, 1)
            gains(0, KT)
            dve.wait_ge(mod_step, 2)

            def normalise(q, x_norm, r, dst_h, dst_l, shift):
                for t in range(KT + 1):
                    if t < KT:
                        if t >= 2:
                            dve.wait_ge(hl_done, KT * q + t - 1)
                        nc.vector.scalar_tensor_tensor(x_norm[:, t % 2], xT[:, t], gain[:, q, t:t + 1], r[:],
                                                       ALU.mult, ALU.mult).then_inc(xn_done, 1)
                    if t >= 1:
                        dve.wait_ge(hh_done, KT * q + t)
                        nc.vector.scalar_tensor_tensor(dst_l[:, t - 1], x_norm[:, (t - 1) % 2],
                                                       mod[:, shift + t - 1:shift + t], dst_h[:, t - 1].bitcast(F32),
                                                       ALU.add, ALU.subtract).then_inc(hl_done, 1)

            def split_l(ready, value, src, high, dst, done):
                dve.wait_ge(ready, value)
                nc.vector.tensor_tensor(dst, src, high.bitcast(F32), ALU.subtract).then_inc(done, 1)

            def split_qkv(n, s):
                split_l(h_ready, STRIPS * n + s + 1, raw[:, s % RING], wh[:, s % RING], wl[:, s % RING], l_ready)

            split_qkv(0, 0)
            dve.sem_inc(masked, 1)
            dve.sem_inc(o_summed, 1)
            normalise(0, xn, rstd, hh, hl, 0)
            split_qkv(0, 1)

            def take_turn(n, use, dst):
                dve.wait_ge(turned[0], turns_before(n) + use + 1)
                nc.vector.tensor_copy(dst, turn[0][:]).then_inc(turn_taken[0], 1)

            def mask_scores(n, d):
                dve.wait_ge(scored, 4 * (n - 1) + d + 1)
                dve.sem_inc(scores_seen, 1)
                side = d // 2
                for b in (2 * (d % 2), 2 * (d % 2) + 1):
                    lo = P if d == 0 and b == 0 else 0
                    for hd in range(2):
                        last = nc.vector.tensor_tensor_reduce(
                            probs[:, hd, side, b, lo:HALF], score[hd][:, HALF * (b % 2) + lo:HALF * (b % 2 + 1)],
                            mask[:, side, lo:HALF], 1.0, MASKED, ALU.add, ALU.max, stat[:, side, b, 0, hd:hd + 1])
                last.then_inc(masked, 1)
                dve.wait_ge(masked, 4 * (n - 1) + d + 2)
                b = 2 * (d % 2)
                nc.vector.tensor_scalar(nmax[:, side, b:b + 2], stat[:, side, b:b + 2, 0], -SCORE_SCALE, None,
                                        ALU.mult).then_inc(nmax_done, 1)

            def body(n, par, project, attend):
                before = 2 if project else 0
                for h in range(HALVES):
                    s = h // 2
                    if project:
                        if h % 2 == 0:
                            split_qkv(n, s + 2)
                        if h in ADA_READ_AT:
                            t = ADA_READ_AT[h]
                            if t % 4 == 0:
                                dve.wait_ge(ada_in, 16 * (2 * n + t // 4 + 1))
                            src = ada_raw[:, t % 4]
                            if t == 0:
                                ins = nc.vector.tensor_scalar(acc[:], src, cond[:, 4, 0:1], None, ALU.mult)
                            else:
                                dve.wait_ge(acc_step, KT * n + t)
                                ins = nc.vector.scalar_tensor_tensor(acc[:], src, cond[:, 4, t:t + 1], acc[:],
                                                                     ALU.mult, ALU.add)
                            ins.then_inc(acc_step, 1)
                        if TURN_V_AT.get(h) in (0, 2):
                            g = TURN_V_AT[h]
                            take_turn(n, g // 2, v_n[:, par, g].rearrange("p b e -> p (b e)"))
                    if attend:
                        if h in SCORE_AT:
                            mask_scores(n, SCORE_AT[h])
                        if h == 8:
                            dve.wait_ge(exp_done, 4 * n)
                            for a in range(4):
                                for b in range(4):
                                    last = nc.vector.tensor_copy(swap[QUAD * b:QUAD * (b + 1), :, a],
                                                                 stat[QUAD * a:QUAD * (a + 1), :, b])
                            last.then_inc(swapped, 1)
                            dve.wait_ge(swapped, n)
                            nc.vector.tensor_tensor(mix[:, 0], swap[:, ::-1, :, 0], stat[:, :, :, 0],
                                                    ALU.max).then_inc(mix_dve, 1)
                            dve.wait_ge(mix_dve, MIX_STEPS * (n - 1) + 1)
                            nc.vector.tensor_tensor(mix[:, 1], stat[:, :, :, 0], mix[:, 0], ALU.subtract).then_inc(mix_dve, 1)
                            nc.vector.tensor_tensor(mix[:, 2], swap[:, ::-1, :, 0], mix[:, 0],
                                                    ALU.subtract).then_inc(mix_dve, 1)
                        if h == 9:
                            dve.wait_ge(mix_act, n)
                            nc.vector.tensor_tensor(mix[:, 5], stat[:, :, :, 1], mix[:, 3], ALU.mult).then_inc(mix_dve, 1)
                            nc.vector.tensor_tensor(mix[:, 6], swap[:, ::-1, :, 1], mix[:, 4], ALU.mult).then_inc(mix_dve, 1)
                            dve.wait_ge(mix_dve, MIX_STEPS * (n - 1) + 5)
                            nc.vector.tensor_tensor(mix[:, 7], mix[:, 5], mix[:, 6], ALU.add).then_inc(mix_dve, 1)
                            dve.wait_ge(mix_dve, MIX_STEPS * (n - 1) + 6)
                            nc.vector.reciprocal(mix[:, 8], mix[:, 7]).then_inc(mix_dve, 1)
                            dve.wait_ge(mix_dve, MIX_STEPS * (n - 1) + 7)
                            nc.vector.tensor_tensor(mix[:, 5], mix[:, 3], mix[:, 8], ALU.mult).then_inc(mix_dve, 1)
                            dve.wait_ge(mix_dve, MIX_STEPS * n)
                            for u in range(8):
                                hd, j = u % 2, u // 2
                                side = j // 2
                                for b in (2 * (j % 2), 2 * (j % 2) + 1):
                                    tile = probs[:, hd, side, b, (P if j == 0 and b == 0 else 0):HALF]
                                    last = nc.vector.tensor_scalar(tile, tile, mix[:, 5, side, b, hd:hd + 1], None, ALU.mult)
                                last.then_inc(scaled, 1)
                        if h in TURN_P_AT:
                            u = 2 * TURN_P_AT[h]
                            take_turn(n, before + u // 2, p_t[:, u % PT_RING])
                    if attend and not project and h in OUT_SPLIT_AT:
                        split_out(split_l, OUT_SPLIT_AT[h], l_ready, wl)
                if attend:
                    dve.wait_ge(oa_copied, n)
                    nat = "p (b j r) -> p b j r"
                    nc.vector.tensor_tensor(o_sum[:].rearrange(nat, b=NT, r=4), o_a[:].rearrange(nat, b=NT, r=4),
                                            o_acc[1][:].rearrange("p (r b j) -> p b j r", b=NT, r=4),
                                            ALU.add).then_inc(o_summed, 1)
                    dve.wait_ge(oh_done, n)
                    at = bass.ds(n - 1, 1)
                    nc.vector.tensor_tensor(ol[:, at].rearrange("p a n -> p (a n)"), o_sum[:],
                                            oh[:, at].rearrange("p a n -> p (a n)").bitcast(F32),
                                            ALU.subtract).then_inc(ol_done, 1)
            bodies(dve, body)

            dve.wait_ge(turn_taken[1], turns_before(PAIRS - 1) + 2)
            modulation(MOD1, MOD)
            dve.wait_ge(mod_step, 3)
            gains(1, 4 * KT)
            dve.wait_ge(mod_step, 4)
            for o in range(OUT_STRIPS):
                dve.wait_ge(strip_done, QKV_STRIPS + o + 1)
                nc.vector.scalar_tensor_tensor(xT[:, o], out_banks[o % 4][:], mod[:, 2 * KT + o:2 * KT + o + 1],
                                               xT[:, o], ALU.mult, ALU.add).then_inc(x1_done, 1)
                if 2 <= o:
                    add_square(o - 1)
                split_ahead(split_l, o, l_ready, fl_ready, wl)
            inverse_root(1, var2, rstd2)
            normalise(1, xn2, rstd2, fh, fl, 3 * KT)

            def gate_branch(f, w):
                dve.wait_ge(gate_done, f + 1)
                dve.wait_ge(fstrip_done, 2 * f + 2)
                nc.vector.tensor_tensor(gate[:], gate[:], banks[2 * w + 1][:], ALU.mult).then_inc(gated, 1)
                dve.wait_ge(act_h_done, f + 1)
                nc.vector.tensor_tensor(tile_of(act_l, f), gate[:], tile_of(act_h, f).bitcast(F32),
                                        ALU.subtract).then_inc(act_l_done, 1)

            def up(i):
                for w in range(2):
                    f = 2 * i + w
                    for u in range(2):
                        split_ffn(split_l, i, 2 * w + u, fl_ready, wl)
                        if u == 0 and not (isinstance(f, int) and f == 0):
                            gate_branch(f - 1, 1 - w)
                        if u == 1:
                            for back, done, before in ((1, tap1_done, tap2_done), (2, tap0_done, tap1_done)):
                                dve.wait_ge(before, f + 1)
                                nc.vector.scalar_tensor_tensor(gate_in[:, back:T], banks[2 * w][:, 0:T - back],
                                                               tap(2 - back, f), gate_in[:, back:T],
                                                               ALU.mult, ALU.add).then_inc(done, 1)
            up(0)
            with dve.Fori(1, FT // 2) as i:
                up(i)
            gate_branch(FT - 1, 1)

            def down(k, u, pair):
                if not (isinstance(k, int) and k >= FT - 3):
                    split_down(split_l, k, u, pair, fl_ready, wl)
            downs(dve, down)

            for o in range(KT):
                dve.wait_ge(y_done, o + 1)
                nc.vector.scalar_tensor_tensor(xT[:, o], banks[(o + 4) % 8][:], mod[:, 5 * KT + o:5 * KT + o + 1],
                                               xT[:, o], ALU.mult, ALU.add).then_inc(x2_done, 1)
            dve.wait_ge(ssq_done, 2 * NT)
            nc.vector.tensor_tensor(rstd_o[:, 0], ssq_o[:, :, 0], ssq_o[:, :, 1], ALU.add).then_inc(rstd_step, 1)
            dve.wait_ge(rstd_step, 1)
            nc.vector.tensor_scalar(rstd_o[:, 1], rstd_o[:, 0], 1.0 / D, EPS, ALU.mult, ALU.add).then_inc(rstd_step, 1)
            dve.wait_ge(rstd_step, 3)
            nc.vector.reciprocal(rstd_o[:, 3], rstd_o[:, 2]).then_inc(rstd_step, 1)
            dve.wait_ge(rstd_step, 4)
            dve.wait_ge(nfin_in, 16)
            for i in range(NT):
                for hf in range(2):
                    nc.vector.scalar_tensor_tensor(out_n[:, i, T * hf:T * (hf + 1)], banks[4 * (1 - hf) + i][:],
                                                   rstd_o[:, 3, i:i + 1], nfin[:, T * hf:T * (hf + 1)],
                                                   ALU.mult, ALU.mult).then_inc(out_done, 1)


_INS = ["x", "c", "w_ada", "b_ada", "norm_mix", "norm_ffn", "attn_w_in", "attn_w_out",
        "ffn_w_up", "ffn_conv_w", "ffn_conv_b", "ffn_w_down", "norm_final"]


def kernel(**inputs):
    import numpy as np
    import concourse.bacc as bacc
    from concourse.bass_utils import run_bass_kernel_spmd

    nc = bacc.Bacc("TRN2", target_bir_lowering=False, num_devices=1)
    arrays, args = {}, []
    for name in _INS:
        a = np.ascontiguousarray(inputs[name])
        arrays[f"in_{name}"] = a
        args.append(nc.dram_tensor(f"in_{name}", a.shape, mybir.dt.from_np(a.dtype), kind="ExternalInput").ap())
    shape = (1, T, D)
    args.append(nc.dram_tensor("out_x", shape, F32, kind="ExternalOutput").ap())
    decoder_layer(nc, *args)
    r = run_bass_kernel_spmd(nc, [arrays], core_ids=[0])
    return r.results[0]["out_x"]
```

```python
from contextlib import ExitStack

import concourse.bass as bass
from concourse import mybir

F32 = mybir.dt.float32
F32R = mybir.dt.float32r
ACT = mybir.ActivationFunctionType
ALU = mybir.AluOpType
AX = mybir.AxisListType

P = 128
T = 512
D = 1024
KT = D // P
NT = T // P
H, E = 16, 64
PAIRS = H // 2
GROUPS = 3
FF = 2816
FT = FF // P
HALF = T // 2
QUAD = 32
EPS = 1e-6
SCORE_SCALE = float(E) ** -0.5
MASKED = -3.0e38
ROOT_STEPS = 6
MIX_STEPS = 8

STRIPS = 3 * GROUPS
RING = 3
QKV_STRIPS = PAIRS * STRIPS
OUT_STRIPS = KT
FRAW, FRING = 2, 4
UP_STRIPS = 2 * FT
PT_RING = 4
MOD = 6 * KT
MOD1 = 2 * KT
HALF_D = D // 2
ADA1 = ((0, 4), (4, 6), (6, 8))
ROWS_A = MOD + 2 * KT
ROWS_B = 4 * FT


def strip_of(s):
    if s < GROUPS:
        return "v", s
    return "qk"[(s - GROUPS) % 2], (s - GROUPS) // 2


def in_order(group, which, src, dst):
    if which == "v" or (group == 0 and which == "k"):
        return src, dst
    if group == 0:
        return (src.rearrange("p (b j r) -> p b j r", b=NT, r=4),
                dst.rearrange("p (b r j) -> p b j r", b=NT, r=4))
    return src.rearrange("p (j r) -> p j r", r=4), dst.rearrange("p (r j) -> p j r", r=4)


def decoder_layer(nc, x, c, w_ada, b_ada, norm_mix, norm_ffn, attn_w_in, attn_w_out,
                  ffn_w_up, ffn_conv_w, ffn_conv_b, ffn_w_down, norm_final, out):
    x_rows = x[0].rearrange("(i p) d -> i p d", p=P)
    out_rows = out[0].rearrange("(i p) d -> i p d", p=P)
    c_cols = c[0].rearrange("(p t) -> p t", t=KT)
    ada = w_ada[0].rearrange("(p t) n -> p t n", t=KT)
    w_qkv = attn_w_in[0].rearrange("(t p) n -> p t n", p=P)
    w_o = attn_w_out[0].rearrange("(t p) n -> p t n", p=P)
    w_up = ffn_w_up[0].rearrange("(t p) n -> p t n", p=P)
    w_down = ffn_w_down[0].rearrange("(f p) n -> f p n", p=P)

    ctx = ExitStack()
    with ctx:
        def tensor(scope, name, shape, dt=F32):
            return scope.enter_context(nc.sbuf_tensor(name, shape, dt))

        def sem(name):
            return ctx.enter_context(nc.semaphore(name))

        xT = tensor(ctx, "xT", [P, KT, T])
        raw = tensor(ctx, "raw", [P, RING, KT, P])
        wh = tensor(ctx, "wh", [P, FRING, KT, P], F32R)
        wl = tensor(ctx, "wl", [P, FRING, KT, P], F32R)
        ident = tensor(ctx, "ident", [P, P])
        ones = tensor(ctx, "ones", [P, P])
        mask = tensor(ctx, "mask", [P, 2, HALF])
        cols_a = tensor(ctx, "cols_a", [P, ROWS_A])
        cols_b = tensor(ctx, "cols_b", [P, ROWS_B])
        mod_raw = tensor(ctx, "mod_raw", [P, MOD])
        mod = tensor(ctx, "mod", [P, MOD])
        gain = tensor(ctx, "gain", [P, 2, KT])
        cond = tensor(ctx, "cond", [P, 5, KT])
        stat = tensor(ctx, "stat", [P, 2, NT, 2, 2])
        swap = tensor(ctx, "swap", [P, 2, NT, 2, 2])
        nmax = tensor(ctx, "nmax", [P, 2, NT, 2])
        mix = tensor(ctx, "mix", [P, 9, 2, NT, 2])
        acc = tensor(ctx, "acc", [P, T])
        warm = tensor(ctx, "warm", [P, 3])
        root = tensor(ctx, "root", [P, ROOT_STEPS + 1, 3 * NT])
        ssq_o = tensor(ctx, "ssq_o", [P, NT, 2])

        scope_a = ExitStack()
        q_t = tensor(scope_a, "q_t", [P, 2, GROUPS, T])
        k_t = tensor(scope_a, "k_t", [P, 2, GROUPS, T])
        v_n = tensor(scope_a, "v_n", [P, 2, GROUPS, NT, P])
        v_t = tensor(scope_a, "v_t", [P, 2, T])
        probs = tensor(scope_a, "probs", [P, 2, 2, NT, HALF])
        p_t = tensor(scope_a, "p_t", [P, PT_RING, T])
        ada_raw = tensor(scope_a, "ada_raw", [P, KT // 2, T])
        o_a = tensor(scope_a, "o_a", [P, T])
        o_sum = tensor(scope_a, "o_sum", [P, T])
        oh = tensor(scope_a, "oh", [P, PAIRS, T], F32R)
        ol = tensor(scope_a, "ol", [P, PAIRS, T], F32R)
        hh = tensor(scope_a, "hh", [P, KT, T], F32R)
        hl = tensor(scope_a, "hl", [P, KT, T], F32R)
        scope_a.close()
        scope_s = ExitStack()
        ada1 = tensor(scope_s, "ada1", [P, KT, 2 * HALF_D])
        acc1 = tensor(scope_s, "acc1", [P, MOD1 * P])
        x_nat = tensor(scope_s, "x_nat", [P, NT, D])
        xr_nat = tensor(scope_s, "xr_nat", [P, NT, D])
        xr = tensor(scope_s, "xr", [P, KT, T])
        rows_a = tensor(scope_s, "rows_a", [ROWS_A, P])
        rows_b = tensor(scope_s, "rows_b", [ROWS_B, P])
        xn = tensor(scope_s, "xn", [P, 2, T])
        same = tensor(scope_s, "same", [4, P])
        scope_s.close()
        scope_f = ExitStack()
        sq2 = tensor(scope_f, "sq2", [P, 2, T])
        sq_sum = tensor(scope_f, "sq_sum", [P, T])
        diag = tensor(scope_f, "diag", [P, T])
        xn2 = tensor(scope_f, "xn2", [P, 2, T])
        fh = tensor(scope_f, "fh", [P, KT, T], F32R)
        fl = tensor(scope_f, "fl", [P, KT, T], F32R)
        act_h = tensor(scope_f, "act_h", [P, FT, T], F32R)
        act_l = tensor(scope_f, "act_l", [P, FT, T], F32R)
        gate_in = tensor(scope_f, "gate_in", [P, T])
        gate = tensor(scope_f, "gate", [P, T])
        scope_f.close()
        scope_g = ExitStack()
        tensor(scope_g, "below_act_h", [P, (2 + 1 + 1 + 2 + 2 * KT) * T])
        wh_first = tensor(scope_g, "wh_first", [P, 2, KT, P], F32R)
        wl_first = tensor(scope_g, "wl_first", [P, 2, KT, P], F32R)
        scope_g.close()
        scope_e = ExitStack()
        out_n = tensor(scope_e, "out_n", [P, NT, D])
        nfin = tensor(scope_e, "nfin", [P, D])
        scope_e.close()

        banks = [ctx.enter_context(nc.psum_tensor(f"bank{i}", [P, T], F32)) for i in range(8)]
        proj, score, turn, o_acc = banks[0:2], banks[2:4], banks[4:6], banks[6:8]
        squares = banks[5]

        x_in = [sem(f"x_in{i}") for i in range(NT)]
        c_in, rows_in, nfin_in = sem("c_in"), sem("rows_in"), sem("nfin_in")
        ada1_in = [sem(f"ada1_in{i}") for i in range(KT)]
        raw_in = [sem(f"raw_in{i}") for i in range(RING)]
        ada_in = sem("ada_in")
        const_done = sem("const_done")
        cond_step, mod_step = sem("cond_step"), sem("mod_step")
        acc1_step, weighted, pool_acc1_step = sem("acc1_step"), sem("weighted"), sem("pool_acc1_step")
        start_turned = sem("start_turned")
        start_taken = sem("start_taken")
        sq_done, sq_summed, sq_added = sem("sq_done"), sem("sq_summed"), sem("sq_added")
        row_squares = sem("row_squares")
        norm_step, root_done = sem("norm_step"), sem("root_done")
        xr_done, diag_done, spread_done = sem("xr_done"), sem("diag_done"), sem("spread_done")
        xn_done = sem("xn_done")
        hh_done, hl_done = sem("hh_done"), sem("hl_done")
        mod1_done, mod1_taken = sem("mod1_done"), sem("mod1_taken")
        same_done = sem("same_done")
        h_ready, l_ready = sem("h_ready"), sem("l_ready")
        strip_done, strip_taken = sem("strip_done"), sem("strip_taken")
        tail_done = sem("tail_done")
        acc_step = sem("acc_step")
        y_done = sem("y_done")
        turned = [sem("turned0"), sem("turned1")]
        turn_taken = [sem("turn_taken0"), sem("turn_taken1")]
        scored, masked, nmax_done, exp_done = sem("scored"), sem("masked"), sem("nmax_done"), sem("exp_done")
        swapped, mix_dve, mix_act = sem("swapped"), sem("mix_dve"), sem("mix_act")
        scaled, pv_done = sem("scaled"), sem("pv_done")
        oa_copied, o_summed, oh_done, ol_done = sem("oa_copied"), sem("o_summed"), sem("oh_done"), sem("ol_done")
        x1_done = sem("x1_done")
        scores_seen, strip_seen = sem("scores_seen"), sem("strip_seen")
        fraw_in = [sem(f"fraw_in{i}") for i in range(FRAW)]
        fh_ready, fl_ready, fstrip_done = sem("fh_ready"), sem("fl_ready"), sem("fstrip_done")
        tap2_done, tap1_done, tap0_done = sem("tap2_done"), sem("tap1_done"), sem("tap0_done")
        gate_done, gated, act_h_done, act_l_done = sem("gate_done"), sem("gated"), sem("act_h_done"), sem("act_l_done")
        x2_done, nat_done, ssq_done, rstd_step, out_done, stored = (
            sem("x2_done"), sem("nat_done"), sem("ssq_done"), sem("rstd_step"), sem("out_done"), sem("stored"))

        block = ctx.enter_context(nc.Block())

        def turns_before(n):
            return 0 if isinstance(n, int) and n == 0 else 6 * n - 4

        SCORE_AT = {0: 0, 2: 1, 4: 2, 6: 3}
        TURN_V_AT = {3: 0, 5: 1, 7: 2}
        ADA_READ_AT = {0: 0, 1: 1, 2: 2, 3: 3, 5: 4, 6: 5, 7: 6, 8: 7}
        ADA_AT = 10
        TURN_P_AT = {12: 0, 14: 1, 15: 2, 16: 3}
        PV_AT = {14: 0, 15: 1, 16: 2, 17: 3}
        HALVES = 2 * STRIPS
        TURN_V_FIRST = {6: 0, 7: 1, 8: 2}
        ADA_READ_FIRST = {4: 0, 5: 1, 6: 2, 7: 3, 12: 4, 13: 5, 14: 6, 15: 7}
        ADA_FIRST = 17
        FILL_AT = {1: 3, 3: 3, 5: 3, 7: 11, 12: 1, 14: 1, 15: 1, 16: 1, 17: 4}
        OUT_AHEAD = 4
        out_banks = banks[0:OUT_AHEAD]
        fill_steps = [(o, t) for o in range(OUT_AHEAD) for t in range(KT - 1)]
        X1_STEPS = ([(o, slice(0, T)) for o in range(OUT_AHEAD)] +
                    [(o, slice(HALF * hf, HALF * (hf + 1))) for hf in range(2) for o in range(OUT_AHEAD, OUT_STRIPS)])

        def start_bank(c, g):
            return banks[(5 + g, 7, 4)[c]]

        def is_first(n):
            return isinstance(n, int) and n == 0

        def is_last(n):
            return isinstance(n, int) and n == PAIRS - 1

        def qkv_bank(n, par, s):
            return banks[2] if is_first(n) and s == 2 else proj[(par + s) % 2]

        def qkv_slot(n, s):
            return RING if is_first(n) and s == RING else s % RING

        def split_at(n, h):
            if h % 2:
                return None
            if is_first(n) and h < 8:
                return h // 2 + 3 if h < 6 else None
            return h // 2 + 2

        def out_slot(o):
            return {2: 3, 3: 2}.get(o, o % FRING)

        def ada1_slice(c, t):
            return ada1[:, t] if c == 0 else ada1[:, 4 * (c - 1) + t // 2, HALF_D * (t % 2):HALF_D * (t % 2 + 1)]

        def of_tiles(t, lo, hi):
            return t[:, 0:MOD1].rearrange("p (g t) -> p g t", g=2)[:, :, lo:hi]

        def columns(eng, at, n):
            return slice(at, at + n) if isinstance(at, int) else bass.ds(at, n)

        def bodies(eng, body):
            body(0, 0, True, False)
            with eng.Fori(0, (PAIRS - 2) // 2) as m:
                body(2 * m + 1, 1, True, True)
                body(2 * m + 2, 0, True, True)
            body(PAIRS - 1, 1, True, True)
            body(PAIRS, 0, False, True)

        def p_blocks(j):
            tiles = (2 * (j % 2), 2 * (j % 2) + 1)
            return [(b, part) for b in tiles for part in range(2) if not (j == 0 and b == 0 and part == 0)]

        def tile_of(t, f):
            at = slice(f, f + 1) if isinstance(f, int) else bass.ds(f, 1)
            return t[:, at].rearrange("p a n -> p (a n)")

        def tap(k, f):
            return cols_b[:, FT * k + f:FT * k + f + 1] if isinstance(f, int) else cols_b[:, bass.ds(FT * k + f, 1)]

        def split_slot(split, j, u, value, ready, dst):
            slot = u % FRING
            if dst is wh:
                if isinstance(j, int) and j < FRING:
                    free = (tail_done, FRING + j + 1)
                else:
                    free = (fstrip_done, j - FRING + 1)
                split(fraw_in[u % FRAW], value, raw[:, u % FRAW], wh[:, slot], free, ready)
            else:
                split(fh_ready, j + 1, raw[:, u % FRAW], wh[:, slot], wl[:, slot], ready)

        def split_ffn(split, i, u, ready, dst):
            split_slot(split, 4 * i + u + 3, (u + 3) % FRING, 16 * (2 * i + (u + 3) // 2 + 1), ready, dst)

        def split_down(split, k, u, pair, ready, dst):
            split_slot(split, UP_STRIPS + k + 3, (u + 3) % FRING, 16 * (UP_STRIPS // 2 + pair + 2 + u % 2), ready, dst)

        def split_out(split, o, ready, dst):
            g = QKV_STRIPS + o
            if dst is wh:
                last = {2: None, 3: QKV_STRIPS, 6: QKV_STRIPS + 4, 7: QKV_STRIPS + 3}.get(o, g - FRING + 1)
                split(raw_in[g % RING], 16 * (g // RING + 1), raw[:, g % RING], wh[:, out_slot(o)],
                      last and (strip_done, last), ready)
            else:
                split(h_ready, g + 1, raw[:, g % RING], wh[:, out_slot(o)], wl[:, out_slot(o)], ready)

        def split_first(split, j, ready, dst):
            if dst is wh:
                split(fraw_in[j], 16, raw[:, j], wh_first[:, j], (strip_done, QKV_STRIPS + OUT_AHEAD), ready)
            else:
                split(fh_ready, j + 1, raw[:, j], wh_first[:, j], wl_first[:, j], ready)

        def downs(eng, down):
            down(0, 0, 0)
            down(1, 1, 0)
            with eng.Fori(0, (FT - 6) // 4) as m:
                for u in range(4):
                    down(4 * m + 2 + u, (2 + u) % FRING, 2 * m + 1 + u // 2)
            for k in range(FT - 4, FT):
                down(k, k % FRING, k // 2)

        @block.sync
        def _(sp):
            sp.dma_start(cond[:, 0, :], c_cols).then_inc(c_in, 16)
            for i in range(NT):
                sp.dma_start(x_nat[:, i, :], x_rows[i]).then_inc(x_in[i], 16)
            ada1_src = ada[:, :, 0:MOD1 * P].rearrange("p t (g n) -> p t g n", g=2)
            for t in range(KT):
                sp.dma_start(ada1[:, t].rearrange("p (g n) -> p g n", g=2), ada1_src[:, t, :, 0:HALF_D]
                             ).then_inc(ada1_in[t], 16)
            for s in range(RING):
                sp.dma_start(raw[:, s], w_qkv[:, :, 2 * GROUPS * D + s * D:2 * GROUPS * D + s * D + P]
                             ).then_inc(raw_in[s], 16)
            for c in (1, 2):
                lo, hi = ADA1[c]
                for t in range(KT):
                    sp.wait_ge(acc1_step, 4 * (c - 1) + t // 2 + 1)
                    sp.dma_start(ada1_slice(c, t).rearrange("p (g n) -> p g n", g=2), ada1_src[:, t, :, P * lo:P * hi]
                                 ).then_inc(ada1_in[4 * (c - 1) + t // 2], 16)

            def load_strips(n, first):
                for s in range(RING if first else 0, STRIPS):
                    kind, g = strip_of(s)
                    at = {"q": 0, "k": 1, "v": 2}[kind] * GROUPS * D + g * D
                    src = w_qkv[:, :, columns(sp, at + P * n, P)]
                    ada_loads = (4, 7) if first else (2, 5)
                    if s in ada_loads:
                        half = ada_loads.index(s)
                        src_ada = ada[:, half * KT // 2:(half + 1) * KT // 2, columns(sp, MOD1 * P + T * n, T)]
                    sp.wait_ge(h_ready, STRIPS * n + s - RING + 1)
                    sp.wait_ge(l_ready, STRIPS * n + s - RING + 1)
                    if at == 0:
                        sp.sem_inc(strip_seen, 1)
                    sp.dma_start(raw[:, s % RING], src).then_inc(raw_in[s % RING], 16)
                    if s in ada_loads:
                        if not (first and half == 0):
                            sp.wait_ge(acc_step, KT * n + 4 * half)
                        elif first:
                            sp.wait_ge(hl_done, KT)
                        sp.dma_start(ada_raw[:], src_ada).then_inc(ada_in, 16)
            load_strips(0, True)
            with sp.Fori(1, PAIRS) as n:
                load_strips(n, False)
            for o in range(OUT_STRIPS):
                g = QKV_STRIPS + o
                sp.wait_ge(h_ready, g - RING + 1)
                sp.wait_ge(l_ready, g - RING + 1)
                sp.dma_start(raw[:, g % RING], w_o[:, :, P * o:P * (o + 1)]).then_inc(raw_in[g % RING], 16)

            def up_columns(f, u):
                return w_up[:, :, columns(sp, FF * u + P * f, P)]
            for j in range(FRAW):
                sp.wait_ge(h_ready, QKV_STRIPS + OUT_STRIPS - 1 + j)
                sp.wait_ge(l_ready, QKV_STRIPS + OUT_STRIPS - 1 + j)
                sp.dma_start(raw[:, j], up_columns(0, j)).then_inc(fraw_in[j], 16)
            with sp.Fori(1, FT) as f:
                for u in range(2):
                    src = up_columns(f, u)
                    sp.wait_ge(fh_ready, 2 * f + u - FRAW + 1)
                    sp.wait_ge(fl_ready, 2 * f + u - FRAW + 1)
                    sp.dma_start(raw[:, u], src).then_inc(fraw_in[u], 16)
            with sp.Fori(0, FT // 2) as m:
                for u in range(2):
                    j = UP_STRIPS + 2 * m + u
                    src = w_down[columns(sp, 2 * m + u, 1)].rearrange("a p n -> p (a n)")
                    sp.wait_ge(fh_ready, j - FRAW + 1)
                    sp.wait_ge(fl_ready, j - FRAW + 1)
                    sp.dma_start(raw[:, u].rearrange("p t n -> p (t n)"), src).then_inc(fraw_in[u], 16)
            sp.wait_ge(act_l_done, FT)
            sp.wait_ge(fstrip_done, UP_STRIPS)
            sp.dma_start(nfin[:], norm_final.partition_broadcast(P)).then_inc(nfin_in, 16)
            for i in range(NT):
                sp.wait_ge(out_done, 2 * (i + 1))
                sp.dma_start(out_rows[i], out_n[:, i, :]).then_inc(stored, 16)
            sp.wait_ge(stored, 16 * NT)

        @block.gpsimd
        def _(pool):
            nc.gpsimd.memset(ident[:], 0.0).then_inc(const_done, 1)
            nc.gpsimd.memset(ones[:], 1.0).then_inc(const_done, 1)
            nc.gpsimd.memset(mask[:], 0.0).then_inc(const_done, 1)
            nc.gpsimd.memset(same[:], 0.0).then_inc(const_done, 1)
            pool.wait_ge(const_done, 4)
            nc.gpsimd.affine_select(out=ident[:], in_=ident[:], compare_op=ALU.not_equal, fill=1.0, base=0,
                                    pattern=[[-1, P]], channel_multiplier=1).then_inc(const_done, 1)
            view = same[:].rearrange("p (a i) -> p a i", i=4)
            nc.gpsimd.affine_select(out=view, in_=view, compare_op=ALU.not_equal, fill=1.0, base=0,
                                    pattern=[[0, P // 4], [-1, 4]], channel_multiplier=1).then_inc(const_done, 1)
            pool.wait_ge(const_done, 6)
            for r in range(4):
                if r:
                    pool.wait_ge(const_done, 6 + 2 * r)
                part = mask[QUAD * r:QUAD * (r + 1), 0]
                nc.gpsimd.affine_select(out=part[:, 0:P], in_=part[:, 0:P], compare_op=ALU.is_ge, fill=MASKED,
                                        base=-r, pattern=[[1, P]], channel_multiplier=-4).then_inc(const_done, 1)
                nc.gpsimd.affine_select(out=part[:, P:HALF], in_=part[:, P:HALF], compare_op=ALU.is_ge, fill=MASKED,
                                        base=r, pattern=[[-1, P]], channel_multiplier=4).then_inc(const_done, 1)
            pool.wait_ge(const_done, 14)
            for g in range(2):
                part = mask[:, 1, P * g:P * (g + 1)]
                nc.gpsimd.affine_select(out=part, in_=part, compare_op=ALU.is_ge, fill=MASKED,
                                        base=0, pattern=[[-1, P]], channel_multiplier=1).then_inc(const_done, 1)
            part = acc1[:, 2 * P * ADA1[1][0]:2 * P * ADA1[1][1]]
            for t in range(1, KT):
                pool.wait_ge(weighted, t + 1)
                if t >= 2:
                    pool.wait_ge(pool_acc1_step, t - 1)
                nc.gpsimd.tensor_tensor(part, ada1_slice(1, 0) if t == 1 else part, ada1_slice(1, t), ALU.add
                                        ).then_inc(pool_acc1_step, 1)

        @block.tensor
        def _(pe):
            pe.wait_ge(const_done, 16)
            for i in range(NT):
                pe.wait_ge(x_in[i], 16)
            for t in range(KT):
                if t >= 4:
                    pe.wait_ge(start_taken, t - 3)
                for i in range(NT):
                    last = nc.tensor.transpose(banks[t % 4][:, P * i:P * (i + 1)], x_nat[:, i, P * t:P * (t + 1)], ident[:])
                last.then_inc(start_turned, 1)
            pe.wait_ge(rows_in, 5 * 16)
            nc.tensor.transpose(banks[4][:, 0:ROWS_A], rows_a[:], ident[0:ROWS_A, 0:ROWS_A])
            nc.tensor.transpose(banks[4][:, P:P + ROWS_B], rows_b[:], ident[0:ROWS_B, 0:ROWS_B]).then_inc(start_turned, 1)
            nc.tensor.matmul(banks[7][:, 0:P], same[:], same[:], start=True, stop=True).then_inc(same_done, 1)

            pe.wait_ge(xr_done, NT)
            for t in range(KT):
                pe.wait_ge(start_taken, KT + 2 + t - 3 if t >= 4 else KT - 3 + t)
                for i in range(NT):
                    last = nc.tensor.transpose(banks[t % 4][:, P * i:P * (i + 1)], xr_nat[:, i, P * t:P * (t + 1)], ident[:])
                last.then_inc(start_turned, 1)

            def start_modulation(c):
                lo, hi = ADA1[c]
                if c == 1:
                    pe.wait_ge(pool_acc1_step, KT - 1)
                else:
                    pe.wait_ge(acc1_step, KT * (1 + c // 2))
                for i in range(2 * (hi - lo)):
                    at = P * (2 * lo + i)
                    last = nc.tensor.transpose(start_bank(c, i // 4)[:, P * (i % 4):P * (i % 4 + 1)], acc1[:, at:at + P],
                                               ident[:])
                last.then_inc(mod1_done, 1)

            def start_strips(tiles):
                for s, t in [(s, t) for t in tiles for s in range(RING)]:
                    if t == 0:
                        pe.wait_ge(l_ready, s + 1)
                    if s == 0:
                        pe.wait_ge(hl_done, t + 1)
                    bank = qkv_bank(0, 0, s)
                    if t == 0:
                        pe.wait_ge(start_taken, 2 * KT + 2)
                    nc.tensor.matmul(bank[:], wl[:, s, t], hh[:, t], start=(t == 0), stop=False)
                    nc.tensor.matmul(bank[:], wh[:, s, t], hh[:, t], start=False, stop=False)
                    last = nc.tensor.matmul(bank[:], wh[:, s, t], hl[:, t], start=False, stop=(t == KT - 1))
                    if t == KT - 1:
                        last.then_inc(strip_done, 1)
            start_modulation(0)
            start_strips(range(0, 3))
            start_modulation(1)
            start_strips(range(3, 5))
            start_modulation(2)
            start_strips(range(5, KT))

            def half_strip(bank, slot, half, xh, xl):
                for t in range(half * KT // 2, (half + 1) * KT // 2):
                    nc.tensor.matmul(bank[:], wl[:, slot, t], xh[:, t], start=(t == 0), stop=False)
                    nc.tensor.matmul(bank[:], wh[:, slot, t], xh[:, t], start=False, stop=False)
                    last = nc.tensor.matmul(bank[:], wh[:, slot, t], xl[:, t], start=False, stop=(t == KT - 1))
                return last

            def make_scores(n, par, d):
                if d == 0:
                    pe.wait_ge(strip_taken, STRIPS * n)
                pe.wait_ge(masked, 4 * (n - 1) + d + 1)
                side, tiles = d // 2, (2 * (d % 2), 2 * (d % 2) + 1)
                for b in tiles:
                    at = HALF * (b % 2)
                    if side == 0:
                        lo = P * max(b - 1, 0)
                        for hd in range(2):
                            e = slice(E * hd, E * (hd + 1))
                            last = nc.tensor.matmul(score[hd][:, at + (P if b == 0 else 0):at + HALF],
                                                    q_t[e, par, 0, P * b:P * (b + 1)],
                                                    k_t[e, par, 0, lo:P * (b + 1)], start=True, stop=True)
                    else:
                        for g in (1, 2):
                            for hd in range(2):
                                e = slice(E * hd, E * (hd + 1))
                                last = nc.tensor.matmul(score[hd][:, at + P * (g - 1):at + P * g],
                                                        q_t[e, par, g, P * b:P * (b + 1)],
                                                        k_t[e, par, g, P * b:P * (b + 1)], start=True, stop=True)
                last.then_inc(scored, 1)

            def turn_values(n, par, g):
                k, use = g % 2, g // 2
                pe.wait_ge(strip_taken, STRIPS * n + g + 1)
                if not (isinstance(n, int) and n == 0 and use == 0):
                    pe.wait_ge(turn_taken[k], turns_before(n) + use)
                src = v_t[:, (par + g) % 2]
                for b in range(NT):
                    keys = src[:, P * b:P * (b + 1)] if g == 0 else src[:, b:T:4]
                    last = nc.tensor.transpose(turn[k][:, P * b:P * (b + 1)], keys, ident[:])
                last.then_inc(turned[k], 1)

            def sum_ada(n):
                pe.wait_ge(acc_step, KT * (n + 1))
                pe.wait_ge(turn_taken[1], turns_before(n) + 1)
                for j in range(NT):
                    last = nc.tensor.transpose(turn[1][:, P * j:P * (j + 1)], acc[:, P * j:P * (j + 1)], ident[:])
                last.then_inc(turned[1], 1)

            def turn_probs(n, u, before):
                hd, j, k = u % 2, u // 2, u % 2
                pe.wait_ge(scaled, 8 * (n - 1) + u + 1)
                pe.wait_ge(turn_taken[k], turns_before(n) + before + j)
                for i, (b, part) in enumerate(p_blocks(j)):
                    last = nc.tensor.transpose(turn[k][:, P * i:P * (i + 1)],
                                               probs[:, hd, j // 2, b, P * part:P * (part + 1)], ident[:])
                last.then_inc(turned[k], 1)

            def weigh_values(n, par, u, before):
                hd, j, k = u % 2, u // 2, u % 2
                e = slice(E * hd, E * (hd + 1))
                pe.wait_ge(turn_taken[k], turns_before(n) + before + j + 1)
                if u == 0:
                    pe.wait_ge(o_summed, n)
                side = j // 2
                blocks = p_blocks(j)
                for i, (b, part) in enumerate(blocks):
                    if side == 0:
                        values = v_n[:, par, 0, b - 1 + part, e]
                    else:
                        values = v_n[:, par, 1 + part, b, e]
                    first = i == 0 or blocks[i - 1][0] != b
                    final = i == len(blocks) - 1 or blocks[i + 1][0] != b
                    last = nc.tensor.matmul(o_acc[side][e, P * b:P * (b + 1)], values, p_t[:, u % PT_RING, P * i:P * (i + 1)],
                                            start=first, stop=final)
                last.then_inc(pv_done, 1)

            def out_tiles(o, tiles, tokens=slice(0, T)):
                bank, slot = out_banks[o % 4], out_slot(o)
                for t in tiles:
                    nc.tensor.matmul(bank[:, tokens], wl[:, slot, t], oh[:, t, tokens], start=(t == 0), stop=False)
                    nc.tensor.matmul(bank[:, tokens], wh[:, slot, t], oh[:, t, tokens], start=False, stop=False)
                    last = nc.tensor.matmul(bank[:, tokens], wh[:, slot, t], ol[:, t, tokens], start=False,
                                            stop=(t == KT - 1))
                return last

            def sum_squares(hf):
                pe.wait_ge(sq_added, OUT_STRIPS - 1 + (OUT_STRIPS - OUT_AHEAD) * hf)
                for i in (2 * hf, 2 * hf + 1):
                    last = nc.tensor.matmul(squares[:, i:i + 1], sq_sum[:, P * i:P * (i + 1)], ones[:, 0:1],
                                            start=True, stop=True)
                last.then_inc(sq_summed, 1)

            def spread_root(hf):
                pe.wait_ge(diag_done, 2 * (hf + 1))
                nc.tensor.matmul(o_acc[hf][:, 0:HALF], ones[:], diag[:, HALF * hf:HALF * (hf + 1)],
                                 start=True, stop=True).then_inc(spread_done, 1)

            def begin_out(steps):
                for o, t in steps:
                    if t == 0:
                        pe.wait_ge(l_ready, QKV_STRIPS + o + 1)
                        if o < 2:
                            pe.wait_ge(strip_taken, QKV_STRIPS - 1 + o)
                        else:
                            pe.wait_ge(masked, 4 * PAIRS + 1)
                    if o == 0:
                        pe.wait_ge(ol_done, t + 1)
                    out_tiles(o, (t,))

            def body(n, par, project, attend):
                before = 2 if project else 0
                filled = 0
                for h in range(2 * RING if is_first(n) else 0, HALVES):
                    s = h // 2
                    if project:
                        g = STRIPS * n + s
                        if h % 2 == 0:
                            pe.wait_ge(l_ready, g + 1)
                            pe.wait_ge(strip_taken, g - 1)
                        last = half_strip(qkv_bank(n, par, s), qkv_slot(n, s), h % 2, hh, hl)
                        if h % 2 == 1:
                            last.then_inc(strip_done, 1)
                        turn_v_at = TURN_V_FIRST if is_first(n) else TURN_V_AT
                        if h in turn_v_at:
                            turn_values(n, par, turn_v_at[h])
                        if h == (ADA_FIRST if is_first(n) else ADA_AT):
                            sum_ada(n)
                    if attend:
                        if h in SCORE_AT:
                            make_scores(n, 1 - par, SCORE_AT[h])
                        if h in PV_AT:
                            for u in (2 * PV_AT[h], 2 * PV_AT[h] + 1):
                                weigh_values(n, 1 - par, u, before)
                        if h in TURN_P_AT:
                            for u in (2 * TURN_P_AT[h], 2 * TURN_P_AT[h] + 1):
                                turn_probs(n, u, before)
                    if attend and not project and h in FILL_AT:
                        begin_out(fill_steps[filled:filled + FILL_AT[h]])
                        filled += FILL_AT[h]
            bodies(pe, body)

            pe.wait_ge(ol_done, PAIRS)
            for o in range(OUT_AHEAD):
                out_tiles(o, (KT - 1,)).then_inc(strip_done, 1)
            for hf in range(2):
                tokens = slice(HALF * hf, HALF * (hf + 1))
                for o in range(OUT_AHEAD, OUT_STRIPS):
                    if hf == 0:
                        pe.wait_ge(l_ready, QKV_STRIPS + o + 1)
                    pe.wait_ge(x1_done, o - OUT_AHEAD + 1 if hf == 0 else o + 1)
                    out_tiles(o, range(KT), tokens).then_inc(tail_done, 1)
                    if hf == 1 and o == OUT_AHEAD:
                        sum_squares(0)
                    if hf == 1 and o == OUT_STRIPS - 2:
                        spread_root(0)

            pe.wait_ge(fl_ready, 2)
            for hf in range(2):
                tokens = slice(HALF * hf, HALF * (hf + 1))
                for t in range(KT):
                    if hf == 0 and t == 4:
                        sum_squares(1)
                    if hf == 0 and t == 7:
                        spread_root(1)
                    pe.wait_ge(hl_done, KT * (hf + 1) + t + 1)
                    for j in range(2):
                        nc.tensor.matmul(banks[j][:, tokens], wl_first[:, j, t], fh[:, t, tokens], start=(t == 0), stop=False)
                        nc.tensor.matmul(banks[j][:, tokens], wh_first[:, j, t], fh[:, t, tokens], start=False, stop=False)
                        last = nc.tensor.matmul(banks[j][:, tokens], wh_first[:, j, t], fl[:, t, tokens],
                                                start=False, stop=(t == KT - 1))
                        if hf == 1 and t == KT - 1:
                            last.then_inc(fstrip_done, 1)

            def up(i):
                for w in range(2):
                    for u in range(2):
                        j = 4 * i + 2 * w + u
                        f = 2 * i + w
                        if isinstance(j, int) and j < 2:
                            continue
                        pe.wait_ge(fl_ready, j + 1)
                        if u == 0 and not (isinstance(i, int) and i == 0):
                            pe.wait_ge(gated, f - 1)
                        bank, slot = banks[2 * w + u], 2 * w + u
                        for t in range(KT):
                            nc.tensor.matmul(bank[:], wl[:, slot, t], fh[:, t], start=(t == 0), stop=False)
                            nc.tensor.matmul(bank[:], wh[:, slot, t], fh[:, t], start=False, stop=False)
                            last = nc.tensor.matmul(bank[:], wh[:, slot, t], fl[:, t], start=False, stop=(t == KT - 1))
                        last.then_inc(fstrip_done, 1)
            up(0)
            with pe.Fori(1, FT // 2) as i:
                up(i)

            def down(k, u, pair):
                static = isinstance(k, int)
                final, slot = static and k == FT - 1, u
                pe.wait_ge(fl_ready, UP_STRIPS + k + 1)
                pe.wait_ge(act_l_done, k + 1)
                for o in range(KT):
                    if static and k == 0 and o in (4, 6):
                        pe.wait_ge(gated, FT - 1 + (o == 6))
                    start, stop = static and k == 0, final
                    at = slice(k, k + 1) if static else bass.ds(k, 1)
                    xh = act_h[:, at].rearrange("p a n -> p (a n)")
                    xl = act_l[:, at].rearrange("p a n -> p (a n)")
                    y = banks[(o + 4) % 8]
                    nc.tensor.matmul(y[:], wl[:, slot, o], xh, start=start, stop=False)
                    nc.tensor.matmul(y[:], wh[:, slot, o], xh, start=False, stop=False)
                    last = nc.tensor.matmul(y[:], wh[:, slot, o], xl, start=False, stop=stop)
                    if final:
                        last.then_inc(y_done, 1)
                if not final:
                    last.then_inc(fstrip_done, 1)
            downs(pe, down)

            for hf in range(2):
                pe.wait_ge(x2_done, KT // 2 * (hf + 1))
                for i in range(NT):
                    for o in range(4):
                        last = nc.tensor.transpose(banks[4 * (1 - hf) + i][:, P * o:P * (o + 1)],
                                                   xT[:, 4 * hf + o, P * i:P * (i + 1)], ident[:])
                    last.then_inc(nat_done, 1)

        @block.scalar
        def _(act):
            act.dma_start(rows_a[0:MOD], b_ada[0].rearrange("(r p) -> r p", p=P)).then_inc(rows_in, 16)
            act.dma_start(rows_a[MOD:MOD + KT], norm_mix[0].rearrange("(r p) -> r p", p=P)).then_inc(rows_in, 16)
            act.dma_start(rows_a[MOD + KT:ROWS_A], norm_ffn[0].rearrange("(r p) -> r p", p=P)).then_inc(rows_in, 16)
            act.dma_start(rows_b[0:3 * FT], ffn_conv_w[0].rearrange("k (r p) -> (k r) p", p=P)).then_inc(rows_in, 16)
            act.dma_start(rows_b[3 * FT:ROWS_B], ffn_conv_b[0].rearrange("(r p) -> r p", p=P)).then_inc(rows_in, 16)
            act.wait_ge(c_in, 16)
            nc.scalar.activation(cond[:, 1], cond[:, 0], ACT.Exp, scale=-1.0).then_inc(cond_step, 1)

            for i in range(NT):
                act.wait_ge(x_in[i], 16)
                nc.scalar.activation(xr_nat[:, i], x_nat[:, i], ACT.Square, accum_out=root[:, 0, i:i + 1]
                                     ).then_inc(row_squares, 1)
            act.wait_ge(const_done, 4)
            nc.scalar.activation(warm[:, 2:3], ones[:, 0:1], ACT.Sqrt)

            def root_of(q, lo, hi):
                act.wait_ge(norm_step, ROOT_STEPS * q + 1)
                nc.scalar.activation(root[:, 2, lo:hi], root[:, 1, lo:hi], ACT.Sqrt).then_inc(root_done, 1)
            root_of(0, 0, NT)
            for t in range(KT):
                act.wait_ge(start_turned, t + 1)
                nc.scalar.activation(xT[:, t], banks[t % 4][:], ACT.Copy).then_inc(start_taken, 1)
            act.wait_ge(start_turned, KT + 1)
            nc.scalar.activation(cols_a[:], banks[4][:, 0:ROWS_A], ACT.Copy).then_inc(start_taken, 1)
            nc.scalar.activation(cols_b[:], banks[4][:, P:P + ROWS_B], ACT.Copy).then_inc(start_taken, 1)
            for t in range(KT):
                act.wait_ge(start_turned, KT + 2 + t)
                nc.scalar.activation(xr[:, t], banks[t % 4][:], ACT.Copy).then_inc(start_taken, 1)

            def split_h(sem_in, value, src, dst, free, done):
                act.wait_ge(sem_in, value)
                if free is not None:
                    act.wait_ge(*free)
                nc.scalar.activation(dst, src, ACT.Copy).then_inc(done, 1)

            def split_qkv(n, s):
                g = STRIPS * n + s
                free = None if isinstance(g, int) and g <= RING else (strip_done, g - RING + 1)
                slot = qkv_slot(n, s)
                split_h(raw_in[s % RING], 16 * (GROUPS * n + s // RING + 1), raw[:, s % RING], wh[:, slot],
                        free, h_ready)


            def weigh_ada1(t):
                act.wait_ge(ada1_in[t // 2], 48)
                for k in (t, t + 1):
                    nc.scalar.activation(ada1_slice(1, k), ada1_slice(1, k), ACT.Copy, scale=cond[:, 4, k:k + 1]
                                         ).then_inc(weighted, 1)

            for s in range(RING):
                split_qkv(0, s)
            for c, (lo, hi) in enumerate(ADA1):
                act.wait_ge(mod_step, 2 * (c + 1))
                for t in range(lo, hi):
                    nc.scalar.activation(hh[:, t], xr[:, t], ACT.Identity, bias=mod[:, t:t + 1],
                                         scale=gain[:, 0, t:t + 1]).then_inc(hh_done, 1)
                    if c == 0:
                        weigh_ada1(2 * t)

            def take_turn(n, use, dst):
                act.wait_ge(turned[1], turns_before(n) + use + 1)
                nc.scalar.activation(dst, turn[1][:], ACT.Copy).then_inc(turn_taken[1], 1)

            def body(n, par, project, attend):
                before = 2 if project else 0
                for h in range(HALVES):
                    s = h // 2
                    if project:
                        if split_at(n, h) is not None:
                            split_qkv(n, split_at(n, h))
                        if h % 2 == 1:
                            act.wait_ge(strip_done, STRIPS * n + s + 1)
                            kind, g = strip_of(s)
                            if is_first(n) and s == 2:
                                act.wait_ge(turned[0], 1)
                            dst = {"v": v_t[:, (par + g) % 2], "q": q_t[:, par, g], "k": k_t[:, par, g]}[kind]
                            src, dst = in_order(g, kind, qkv_bank(n, par, s)[:], dst)
                            nc.scalar.activation(dst, src, ACT.Copy).then_inc(strip_taken, 1)
                        if (TURN_V_FIRST if is_first(n) else TURN_V_AT).get(h) == 1:
                            take_turn(n, 0, v_n[:, par, 1].rearrange("p b e -> p (b e)"))
                    if attend and not project and h == 0:
                        split_out(split_h, 3, h_ready, wh)
                    if attend:
                        if h in SCORE_AT:
                            d = SCORE_AT[h]
                            act.wait_ge(nmax_done, 4 * (n - 1) + d + 1)
                            side = d // 2
                            for b in (2 * (d % 2), 2 * (d % 2) + 1):
                                for hd in range(2):
                                    tile = probs[:, hd, side, b, (P if d == 0 and b == 0 else 0):HALF]
                                    last = nc.scalar.activation(tile, tile, ACT.Exp, bias=nmax[:, side, b, hd:hd + 1],
                                                                scale=SCORE_SCALE, accum_out=stat[:, side, b, 1, hd:hd + 1])
                            last.then_inc(exp_done, 1)
                        if h == 8:
                            act.wait_ge(mix_dve, MIX_STEPS * (n - 1) + 3)
                            nc.scalar.activation(mix[:, 3:5], mix[:, 1:3], ACT.Exp, scale=SCORE_SCALE).then_inc(mix_act, 1)
                        if h in TURN_P_AT:
                            u = 2 * TURN_P_AT[h] + 1
                            take_turn(n, before + u // 2, p_t[:, u % PT_RING])
                    if is_last(n) and h == HALVES - 2:
                        split_out(split_h, 2, h_ready, wh)
                if attend:
                    act.wait_ge(pv_done, 8 * n)
                    nc.scalar.activation(o_a[:].rearrange("p (b j r) -> p b j r", b=NT, r=4),
                                         o_acc[0][:].rearrange("p (b r j) -> p b j r", b=NT, r=4),
                                         ACT.Copy).then_inc(oa_copied, 1)
                    act.wait_ge(o_summed, n + 1)
                    nc.scalar.activation(oh[:, bass.ds(n - 1, 1)].rearrange("p a n -> p (a n)"), o_sum[:],
                                         ACT.Copy).then_inc(oh_done, 1)
            bodies(act, body)

            nc.scalar.activation(warm[:, 0:1], ones[:, 0:1], ACT.Sqrt)

            def square(e):
                o, tokens = X1_STEPS[e]
                act.wait_ge(x1_done, e + 1)
                if e >= 3:
                    act.wait_ge(sq_added, e - 2)
                nc.scalar.activation(sq2[:, e % 2, tokens] if e else sq_sum[:], xT[:, o, tokens], ACT.Square
                                     ).then_inc(sq_done, 1)

            def high_part(hf, t):
                tokens = slice(HALF * hf, HALF * (hf + 1))
                act.wait_ge(xn_done, KT * (hf + 1) + t + 1)
                nc.scalar.activation(fh[:, t, tokens], xn2[:, t % 2, tokens], ACT.Identity,
                                     bias=mod[:, 3 * KT + t:3 * KT + t + 1]).then_inc(hh_done, 1)

            for o in range(OUT_AHEAD):
                split_out(split_h, OUT_AHEAD + o, h_ready, wh)
                square(o)
            for e in range(4, 8):
                square(e)
                if e == 5:
                    split_first(split_h, 0, fh_ready, wh)
            root_of(1, NT, NT + 2)
            split_first(split_h, 1, fh_ready, wh)
            for e in range(8, 11):
                square(e)
            for t in range(3):
                high_part(0, t)
            square(11)
            for t in range(3, 5):
                high_part(0, t)
            root_of(2, NT + 2, 2 * NT)
            for t in range(5, KT):
                high_part(0, t)
            split_slot(split_h, 2, 2, 32, fh_ready, wh)
            for t in range(KT):
                high_part(1, t)

            def gate_branch(f):
                act.wait_ge(tap0_done, f + 1)
                if not (isinstance(f, int) and f == 0):
                    act.wait_ge(act_l_done, f)
                nc.scalar.activation(gate[:], gate_in[:], ACT.Silu).then_inc(gate_done, 1)
                act.wait_ge(gated, f + 1)
                nc.scalar.activation(tile_of(act_h, f), gate[:], ACT.Copy).then_inc(act_h_done, 1)

            def up(i):
                for w in range(2):
                    f = 2 * i + w
                    for u in range(2):
                        j = 4 * i + 2 * w + u
                        split_ffn(split_h, i, 2 * w + u, fh_ready, wh)
                        if u == 0 and not (isinstance(f, int) and f == 0):
                            gate_branch(f - 1)
                        if u == 1:
                            act.wait_ge(fstrip_done, j)
                            nc.scalar.activation(gate_in[:], banks[2 * w][:], ACT.Identity, bias=tap(3, f),
                                                 scale=tap(2, f)).then_inc(tap2_done, 1)
            up(0)
            with act.Fori(1, FT // 2) as i:
                up(i)
            gate_branch(FT - 1)

            def down(k, u, pair):
                if not (isinstance(k, int) and k >= FT - 3):
                    split_down(split_h, k, u, pair, fh_ready, wh)
            downs(act, down)

            nc.scalar.activation(warm[:, 1:2], ones[:, 0:1], ACT.Sqrt)
            for hf in range(2):
                for i in range(NT):
                    act.wait_ge(nat_done, NT * hf + i + 1)
                    nc.scalar.activation(out_n[:, i, T * hf:T * (hf + 1)], banks[4 * (1 - hf) + i][:], ACT.Square,
                                         accum_out=ssq_o[:, i, hf:hf + 1]).then_inc(ssq_done, 1)
            root_of(3, 2 * NT, 3 * NT)

        @block.vector
        def _(dve):
            dve.wait_ge(cond_step, 1)
            nc.vector.tensor_scalar(cond[:, 2], cond[:, 1], 1.0, None, ALU.add).then_inc(cond_step, 1)
            dve.wait_ge(cond_step, 2)
            nc.vector.reciprocal(cond[:, 3], cond[:, 2]).then_inc(cond_step, 1)
            dve.wait_ge(cond_step, 3)
            nc.vector.tensor_tensor(cond[:, 4], cond[:, 0], cond[:, 3], ALU.mult).then_inc(cond_step, 1)
            dve.wait_ge(cond_step, 4)
            def accumulate(c):
                lo, hi = ADA1[c]
                part = acc1[:, 2 * P * lo:2 * P * hi]
                for t in range(KT):
                    if c == 0:
                        dve.wait_ge(ada1_in[t], 16)
                    elif t % 2 == 0:
                        dve.wait_ge(ada1_in[4 + t // 2], 48)
                    if t == 0:
                        nc.vector.tensor_scalar(part, ada1_slice(c, 0), cond[:, 4, 0:1], None, ALU.mult
                                                ).then_inc(acc1_step, 1)
                    else:
                        dve.wait_ge(acc1_step, KT * (c // 2) + t)
                        nc.vector.scalar_tensor_tensor(part, ada1_slice(c, t), cond[:, 4, t:t + 1], part,
                                                       ALU.mult, ALU.add).then_inc(acc1_step, 1)

            def add_square(e):
                tokens = X1_STEPS[e][1]
                dve.wait_ge(sq_done, e + 1)
                if e >= 2:
                    dve.wait_ge(sq_added, e - 1)
                nc.vector.tensor_tensor(sq_sum[:, tokens], sq_sum[:, tokens], sq2[:, e % 2, tokens], ALU.add
                                        ).then_inc(sq_added, 1)

            def inverse_root(q, sums, lo, hi):
                v, y, r = root[:, 1, lo:hi], root[:, 3, lo:hi], root[:, ROOT_STEPS, lo:hi]
                nc.vector.tensor_scalar(v, sums, 1.0 / D, EPS, ALU.mult, ALU.add).then_inc(norm_step, 1)
                dve.wait_ge(root_done, q + 1)
                nc.vector.reciprocal(y, root[:, 2, lo:hi]).then_inc(norm_step, 1)
                dve.wait_ge(norm_step, ROOT_STEPS * q + 2)
                nc.vector.tensor_tensor(root[:, 4, lo:hi], y, y, ALU.mult).then_inc(norm_step, 1)
                dve.wait_ge(norm_step, ROOT_STEPS * q + 3)
                nc.vector.tensor_tensor(root[:, 5, lo:hi], root[:, 4, lo:hi], v, ALU.mult).then_inc(norm_step, 1)
                dve.wait_ge(norm_step, ROOT_STEPS * q + 4)
                nc.vector.tensor_scalar(root[:, 0, lo:hi], root[:, 5, lo:hi], -0.5, 1.5, ALU.mult, ALU.add
                                        ).then_inc(norm_step, 1)
                dve.wait_ge(norm_step, ROOT_STEPS * q + 5)
                nc.vector.tensor_tensor(r, y, root[:, 0, lo:hi], ALU.mult).then_inc(norm_step, 1)
                dve.wait_ge(norm_step, ROOT_STEPS * (q + 1))

            dve.wait_ge(row_squares, NT)
            inverse_root(0, root[:, 0, 0:NT], 0, NT)

            for i in range(NT):
                nc.vector.tensor_scalar(xr_nat[:, i], x_nat[:, i], root[:, ROOT_STEPS, i:i + 1], None, ALU.mult
                                        ).then_inc(xr_done, 1)
            dve.wait_ge(same_done, 1)
            dve.wait_ge(const_done, 16)
            nc.vector.tensor_scalar(xn[:, 0, 0:P], banks[7][:, 0:P], 1.0, -MASKED, ALU.subtract, ALU.mult
                                    ).then_inc(same_done, 1)
            dve.wait_ge(same_done, 2)
            nc.vector.tensor_tensor(mask[:, 1, P:HALF], mask[:, 1, P:HALF], xn[:, 0, 0:P], ALU.min).then_inc(same_done, 1)
            dve.wait_ge(same_done, 3)

            def split_l(ready, value, src, high, dst, done):
                dve.wait_ge(ready, value)
                nc.vector.tensor_tensor(dst, src, high.bitcast(F32), ALU.subtract).then_inc(done, 1)

            def split_qkv(n, s):
                split_l(h_ready, STRIPS * n + s + 1, raw[:, s % RING], wh[:, qkv_slot(n, s)],
                        wl[:, qkv_slot(n, s)], l_ready)

            dve.sem_inc(masked, 1)
            dve.sem_inc(o_summed, 1)
            def start_gains(c):
                lo, hi = ADA1[c]
                dve.wait_ge(mod1_done, c + 1)
                for g in range(2):
                    w = hi - lo
                    src = start_bank(c, g)[:] if c == 0 else start_bank(c, 0)[:, P * w * g:P * w * (g + 1)]
                    last = nc.vector.tensor_reduce(mod_raw[:, KT * g + lo:KT * g + hi],
                                                   src.rearrange("p (t n) -> p t n", n=P), AX.X, ALU.add)
                last.then_inc(mod1_taken, 1)
                dve.wait_ge(mod1_taken, c + 1)
                dve.wait_ge(start_taken, KT + 2)
                nc.vector.tensor_tensor(of_tiles(mod, lo, hi), of_tiles(mod_raw, lo, hi), of_tiles(cols_a, lo, hi), ALU.add
                                        ).then_inc(mod_step, 1)
                dve.wait_ge(mod_step, 2 * c + 1)
                nc.vector.scalar_tensor_tensor(gain[:, 0, lo:hi], mod[:, KT + lo:KT + hi], 1.0,
                                               cols_a[:, MOD + lo:MOD + hi], ALU.add, ALU.mult).then_inc(mod_step, 1)
                dve.wait_ge(mod_step, 2 * (c + 1))

            def start_tiles(c):
                for t in range(*ADA1[c]):
                    dve.wait_ge(start_taken, KT + 2 + t + 1)
                    if t >= 2:
                        dve.wait_ge(hl_done, t - 1)
                    nc.vector.tensor_scalar(xn[:, t % 2], xr[:, t], gain[:, 0, t:t + 1], mod[:, t:t + 1],
                                            ALU.mult, ALU.add).then_inc(xn_done, 1)
                    dve.wait_ge(xn_done, t + 1)
                    dve.wait_ge(hh_done, t + 1)
                    nc.vector.tensor_tensor(hl[:, t], xn[:, t % 2], hh[:, t].bitcast(F32), ALU.subtract
                                            ).then_inc(hl_done, 1)

            accumulate(0)
            for s in range(RING):
                split_qkv(0, s)
            start_gains(0)
            start_tiles(0)
            accumulate(2)
            start_gains(1)
            start_tiles(1)
            start_gains(2)
            start_tiles(2)

            def take_turn(n, use, dst):
                dve.wait_ge(turned[0], turns_before(n) + use + 1)
                nc.vector.tensor_copy(dst, turn[0][:]).then_inc(turn_taken[0], 1)

            def mask_scores(n, d):
                dve.wait_ge(scored, 4 * (n - 1) + d + 1)
                dve.sem_inc(scores_seen, 1)
                side = d // 2
                for b in (2 * (d % 2), 2 * (d % 2) + 1):
                    lo = P if d == 0 and b == 0 else 0
                    for hd in range(2):
                        last = nc.vector.tensor_tensor_reduce(
                            probs[:, hd, side, b, lo:HALF], score[hd][:, HALF * (b % 2) + lo:HALF * (b % 2 + 1)],
                            mask[:, side, lo:HALF], 1.0, MASKED, ALU.add, ALU.max, stat[:, side, b, 0, hd:hd + 1])
                last.then_inc(masked, 1)
                dve.wait_ge(masked, 4 * (n - 1) + d + 2)
                b = 2 * (d % 2)
                nc.vector.tensor_scalar(nmax[:, side, b:b + 2], stat[:, side, b:b + 2, 0], -SCORE_SCALE, None,
                                        ALU.mult).then_inc(nmax_done, 1)

            def weigh(units):
                for u in units:
                    hd, j = u % 2, u // 2
                    side = j // 2
                    for b in (2 * (j % 2), 2 * (j % 2) + 1):
                        tile = probs[:, hd, side, b, (P if j == 0 and b == 0 else 0):HALF]
                        last = nc.vector.tensor_scalar(tile, tile, mix[:, 5, side, b, hd:hd + 1], None, ALU.mult)
                    last.then_inc(scaled, 1)

            def body(n, par, project, attend):
                before = 2 if project else 0
                for h in range(HALVES):
                    s = h // 2
                    if project:
                        if split_at(n, h) is not None:
                            split_qkv(n, split_at(n, h))
                        ada_read_at = ADA_READ_FIRST if is_first(n) else ADA_READ_AT
                        if h in ada_read_at:
                            t = ada_read_at[h]
                            if t % 4 == 0:
                                dve.wait_ge(ada_in, 16 * (2 * n + t // 4 + 1))
                            src = ada_raw[:, t % 4]
                            if t == 0:
                                ins = nc.vector.tensor_scalar(acc[:], src, cond[:, 4, 0:1], None, ALU.mult)
                            else:
                                dve.wait_ge(acc_step, KT * n + t)
                                ins = nc.vector.scalar_tensor_tensor(acc[:], src, cond[:, 4, t:t + 1], acc[:],
                                                                     ALU.mult, ALU.add)
                            ins.then_inc(acc_step, 1)
                        if h == (ADA_FIRST if is_first(n) else ADA_AT):
                            dve.wait_ge(turned[1], turns_before(n) + 2)
                            nc.vector.tensor_reduce(mod_raw[:, bass.ds(MOD1 + NT * n, NT)],
                                                    turn[1][:].rearrange("p (t n) -> p t n", n=P), AX.X, ALU.add
                                                    ).then_inc(turn_taken[1], 1)
                        g = (TURN_V_FIRST if is_first(n) else TURN_V_AT).get(h)
                        if g in (0, 2):
                            take_turn(n, g // 2, v_n[:, par, g].rearrange("p b e -> p (b e)"))
                    if attend:
                        if h in SCORE_AT:
                            mask_scores(n, SCORE_AT[h])
                        if h == 8:
                            dve.wait_ge(exp_done, 4 * n)
                            for a in range(4):
                                for b in range(4):
                                    last = nc.vector.tensor_copy(swap[QUAD * b:QUAD * (b + 1), :, a],
                                                                 stat[QUAD * a:QUAD * (a + 1), :, b])
                            last.then_inc(swapped, 1)
                            dve.wait_ge(swapped, n)
                            nc.vector.tensor_tensor(mix[:, 0], swap[:, ::-1, :, 0], stat[:, :, :, 0],
                                                    ALU.max).then_inc(mix_dve, 1)
                            dve.wait_ge(mix_dve, MIX_STEPS * (n - 1) + 1)
                            nc.vector.tensor_tensor(mix[:, 1], stat[:, :, :, 0], mix[:, 0], ALU.subtract).then_inc(mix_dve, 1)
                            nc.vector.tensor_tensor(mix[:, 2], swap[:, ::-1, :, 0], mix[:, 0],
                                                    ALU.subtract).then_inc(mix_dve, 1)
                        if h == 9:
                            dve.wait_ge(mix_act, n)
                            nc.vector.tensor_tensor(mix[:, 5], stat[:, :, :, 1], mix[:, 3], ALU.mult).then_inc(mix_dve, 1)
                            nc.vector.tensor_tensor(mix[:, 6], swap[:, ::-1, :, 1], mix[:, 4], ALU.mult).then_inc(mix_dve, 1)
                            dve.wait_ge(mix_dve, MIX_STEPS * (n - 1) + 5)
                            nc.vector.tensor_tensor(mix[:, 7], mix[:, 5], mix[:, 6], ALU.add).then_inc(mix_dve, 1)
                            dve.wait_ge(mix_dve, MIX_STEPS * (n - 1) + 6)
                            nc.vector.reciprocal(mix[:, 8], mix[:, 7]).then_inc(mix_dve, 1)
                            dve.wait_ge(mix_dve, MIX_STEPS * (n - 1) + 7)
                            nc.vector.tensor_tensor(mix[:, 5], mix[:, 3], mix[:, 8], ALU.mult).then_inc(mix_dve, 1)
                            dve.wait_ge(mix_dve, MIX_STEPS * n)
                            weigh(range(4))
                        if h in TURN_P_AT:
                            u = 2 * TURN_P_AT[h]
                            take_turn(n, before + u // 2, p_t[:, u % PT_RING])
                            if u == 0:
                                weigh(range(4, 8))
                    if is_last(n) and h == HALVES - 2:
                        split_out(split_l, 2, l_ready, wl)
                    if attend and not project and h == 0:
                        split_out(split_l, 3, l_ready, wl)
                if attend:
                    dve.wait_ge(oa_copied, n)
                    nat = "p (b j r) -> p b j r"
                    nc.vector.tensor_tensor(o_sum[:].rearrange(nat, b=NT, r=4), o_a[:].rearrange(nat, b=NT, r=4),
                                            o_acc[1][:].rearrange("p (r b j) -> p b j r", b=NT, r=4),
                                            ALU.add).then_inc(o_summed, 1)
                    dve.wait_ge(oh_done, n)
                    at = bass.ds(n - 1, 1)
                    nc.vector.tensor_tensor(ol[:, at].rearrange("p a n -> p (a n)"), o_sum[:],
                                            oh[:, at].rearrange("p a n -> p (a n)").bitcast(F32),
                                            ALU.subtract).then_inc(ol_done, 1)
            bodies(dve, body)

            dve.wait_ge(turn_taken[1], turns_before(PAIRS - 1) + 2)
            nc.vector.tensor_tensor(mod[:, MOD1:MOD], mod_raw[:, MOD1:MOD], cols_a[:, MOD1:MOD], ALU.add
                                    ).then_inc(mod_step, 1)
            dve.wait_ge(mod_step, 7)
            nc.vector.scalar_tensor_tensor(gain[:, 1], mod[:, 4 * KT:5 * KT], 1.0, cols_a[:, MOD + KT:MOD + 2 * KT],
                                           ALU.add, ALU.mult).then_inc(mod_step, 1)
            dve.wait_ge(mod_step, 8)

            def add_attention(e):
                o, tokens = X1_STEPS[e]
                if e < OUT_AHEAD:
                    dve.wait_ge(strip_done, QKV_STRIPS + o + 1)
                else:
                    dve.wait_ge(tail_done, e - OUT_AHEAD + 1)
                nc.vector.scalar_tensor_tensor(xT[:, o, tokens], out_banks[o % 4][:, tokens],
                                               mod[:, 2 * KT + o:2 * KT + o + 1], xT[:, o, tokens],
                                               ALU.mult, ALU.add).then_inc(x1_done, 1)
                if e not in (0, 1, 8):
                    add_square(e - 1)

            def second_root(hf):
                lo = NT + 2 * hf
                dve.wait_ge(sq_summed, hf + 1)
                inverse_root(1 + hf, squares[:, 2 * hf:2 * hf + 2], lo, lo + 2)
                for i in (2 * hf, 2 * hf + 1):
                    nc.vector.tensor_scalar(diag[:, P * i:P * (i + 1)], ident[:], root[:, ROOT_STEPS, NT + i:NT + i + 1],
                                            None, ALU.mult).then_inc(diag_done, 1)

            def second_norm(hf, t):
                tokens = slice(HALF * hf, HALF * (hf + 1))
                done = KT * (hf + 1)
                if t == 0:
                    dve.wait_ge(spread_done, hf + 1)
                if t < KT:
                    if t >= 2:
                        dve.wait_ge(hl_done, done + t - 1)
                    nc.vector.scalar_tensor_tensor(xn2[:, t % 2, tokens], xT[:, t, tokens], gain[:, 1, t:t + 1],
                                                   o_acc[hf][:, 0:HALF], ALU.mult, ALU.mult).then_inc(xn_done, 1)
                if t >= 1:
                    dve.wait_ge(hh_done, done + t)
                    nc.vector.scalar_tensor_tensor(fl[:, t - 1, tokens], xn2[:, (t - 1) % 2, tokens],
                                                   mod[:, 3 * KT + t - 1:3 * KT + t], fh[:, t - 1, tokens].bitcast(F32),
                                                   ALU.add, ALU.subtract).then_inc(hl_done, 1)

            for o in range(OUT_AHEAD):
                add_attention(o)
                split_out(split_l, OUT_AHEAD + o, l_ready, wl)
            for e in range(4, 8):
                add_attention(e)
                if e == 5:
                    split_first(split_l, 0, fl_ready, wl)
            add_square(7)
            second_root(0)
            split_first(split_l, 1, fl_ready, wl)
            for e in range(8, 11):
                add_attention(e)
            for t in range(3):
                second_norm(0, t)
            add_attention(11)
            add_square(11)
            for t in range(3, 5):
                second_norm(0, t)
            second_root(1)
            for t in range(5, KT + 1):
                second_norm(0, t)
            split_slot(split_l, 2, 2, 32, fl_ready, wl)
            for t in range(KT + 1):
                second_norm(1, t)

            def gate_branch(f, w):
                dve.wait_ge(gate_done, f + 1)
                dve.wait_ge(fstrip_done, 2 * f + 2)
                nc.vector.tensor_tensor(gate[:], gate[:], banks[2 * w + 1][:], ALU.mult).then_inc(gated, 1)
                dve.wait_ge(act_h_done, f + 1)
                nc.vector.tensor_tensor(tile_of(act_l, f), gate[:], tile_of(act_h, f).bitcast(F32),
                                        ALU.subtract).then_inc(act_l_done, 1)

            def up(i):
                for w in range(2):
                    f = 2 * i + w
                    for u in range(2):
                        split_ffn(split_l, i, 2 * w + u, fl_ready, wl)
                        if u == 0 and not (isinstance(f, int) and f == 0):
                            gate_branch(f - 1, 1 - w)
                        if u == 1:
                            for back, done, before in ((1, tap1_done, tap2_done), (2, tap0_done, tap1_done)):
                                dve.wait_ge(before, f + 1)
                                nc.vector.scalar_tensor_tensor(gate_in[:, back:T], banks[2 * w][:, 0:T - back],
                                                               tap(2 - back, f), gate_in[:, back:T],
                                                               ALU.mult, ALU.add).then_inc(done, 1)
            up(0)
            with dve.Fori(1, FT // 2) as i:
                up(i)
            gate_branch(FT - 1, 1)

            def down(k, u, pair):
                if not (isinstance(k, int) and k >= FT - 3):
                    split_down(split_l, k, u, pair, fl_ready, wl)
            downs(dve, down)

            for o in range(KT):
                dve.wait_ge(y_done, o + 1)
                nc.vector.scalar_tensor_tensor(xT[:, o], banks[(o + 4) % 8][:], mod[:, 5 * KT + o:5 * KT + o + 1],
                                               xT[:, o], ALU.mult, ALU.add).then_inc(x2_done, 1)
            dve.wait_ge(ssq_done, 2 * NT)
            nc.vector.tensor_tensor(root[:, 0, 2 * NT:3 * NT], ssq_o[:, :, 0], ssq_o[:, :, 1], ALU.add).then_inc(rstd_step, 1)
            dve.wait_ge(rstd_step, 1)
            inverse_root(3, root[:, 0, 2 * NT:3 * NT], 2 * NT, 3 * NT)
            dve.wait_ge(nfin_in, 16)
            for i in range(NT):
                for hf in range(2):
                    nc.vector.scalar_tensor_tensor(out_n[:, i, T * hf:T * (hf + 1)], banks[4 * (1 - hf) + i][:],
                                                   root[:, ROOT_STEPS, 2 * NT + i:2 * NT + i + 1], nfin[:, T * hf:T * (hf + 1)],
                                                   ALU.mult, ALU.mult).then_inc(out_done, 1)


_INS = ["x", "c", "w_ada", "b_ada", "norm_mix", "norm_ffn", "attn_w_in", "attn_w_out",
        "ffn_w_up", "ffn_conv_w", "ffn_conv_b", "ffn_w_down", "norm_final"]


def kernel(**inputs):
    import numpy as np
    import concourse.bacc as bacc
    from concourse.bass_utils import run_bass_kernel_spmd

    nc = bacc.Bacc("TRN2", target_bir_lowering=False, num_devices=1)
    arrays, args = {}, []
    for name in _INS:
        a = np.ascontiguousarray(inputs[name])
        arrays[f"in_{name}"] = a
        args.append(nc.dram_tensor(f"in_{name}", a.shape, mybir.dt.from_np(a.dtype), kind="ExternalInput").ap())
    shape = (1, T, D)
    args.append(nc.dram_tensor("out_x", shape, F32, kind="ExternalOutput").ap())
    decoder_layer(nc, *args)
    r = run_bass_kernel_spmd(nc, [arrays], core_ids=[0])
    return r.results[0]["out_x"]
```

```python
from contextlib import ExitStack

import concourse.bass as bass
from concourse import mybir

F32 = mybir.dt.float32
F32R = mybir.dt.float32r
ACT = mybir.ActivationFunctionType
ALU = mybir.AluOpType
AX = mybir.AxisListType

P = 128
T = 512
D = 1024
KT = D // P
NT = T // P
H, E = 16, 64
PAIRS = H // 2
GROUPS = 3
FF = 2816
FT = FF // P
HALF = T // 2
QUAD = 32
EPS = 1e-6
SCORE_SCALE = float(E) ** -0.5
MASKED = -3.0e38
ROOT_STEPS = 6
MIX_STEPS = 8

STRIPS = 3 * GROUPS
RING = 3
QKV_STRIPS = PAIRS * STRIPS
OUT_STRIPS = KT
FRAW, FRING = 2, 4
UP_STRIPS = 2 * FT
PT_RING = 4
MOD = 6 * KT
MIDDLE = (2, 6)
MOD1 = 2 * KT
ADA1 = ((0, 2), (2, 4), (4, 6), (6, 8))
ROWS_A = MOD + 2 * KT
ROWS_B = 4 * FT


def strip_of(s):
    if s < GROUPS:
        return "v", s
    return "qk"[(s - GROUPS) % 2], (s - GROUPS) // 2


def in_order(group, which, src, dst):
    if which == "v" or (group == 0 and which == "k"):
        return src, dst
    if group == 0:
        return (src.rearrange("p (b j r) -> p b j r", b=NT, r=4),
                dst.rearrange("p (b r j) -> p b j r", b=NT, r=4))
    return src.rearrange("p (j r) -> p j r", r=4), dst.rearrange("p (r j) -> p j r", r=4)


def decoder_layer(nc, x, c, w_ada, b_ada, norm_mix, norm_ffn, attn_w_in, attn_w_out,
                  ffn_w_up, ffn_conv_w, ffn_conv_b, ffn_w_down, norm_final, out):
    x_rows = x[0].rearrange("(i p) d -> i p d", p=P)
    out_rows = out[0].rearrange("(i p) d -> i p d", p=P)
    c_cols = c[0].rearrange("(p t) -> p t", t=KT)
    ada = w_ada[0].rearrange("(p t) n -> p t n", t=KT)
    w_qkv = attn_w_in[0].rearrange("(t p) n -> p t n", p=P)
    w_o = attn_w_out[0].rearrange("(t p) n -> p t n", p=P)
    w_up = ffn_w_up[0].rearrange("(t p) n -> p t n", p=P)
    w_down = ffn_w_down[0].rearrange("(f p) n -> f p n", p=P)

    ctx = ExitStack()
    with ctx:
        def tensor(scope, name, shape, dt=F32):
            return scope.enter_context(nc.sbuf_tensor(name, shape, dt))

        def sem(name):
            return ctx.enter_context(nc.semaphore(name))

        xT = tensor(ctx, "xT", [P, KT, T])
        raw = tensor(ctx, "raw", [P, RING, KT, P])
        wh = tensor(ctx, "wh", [P, FRING, KT, P], F32R)
        wl = tensor(ctx, "wl", [P, FRING, KT, P], F32R)
        ident = tensor(ctx, "ident", [P, P])
        ones = tensor(ctx, "ones", [P, P])
        mask = tensor(ctx, "mask", [P, 2, HALF])
        cols_a = tensor(ctx, "cols_a", [P, ROWS_A])
        cols_b = tensor(ctx, "cols_b", [P, ROWS_B])
        mod_raw = tensor(ctx, "mod_raw", [P, MOD])
        mod = tensor(ctx, "mod", [P, MOD])
        gain = tensor(ctx, "gain", [P, 2, KT])
        cond = tensor(ctx, "cond", [P, 5, KT])
        stat = tensor(ctx, "stat", [P, 2, NT, 2, 2])
        swap = tensor(ctx, "swap", [P, 2, NT, 2, 2])
        nmax = tensor(ctx, "nmax", [P, 2, NT, 2])
        mix = tensor(ctx, "mix", [P, 9, 2, NT, 2])
        acc = tensor(ctx, "acc", [P, T])
        warm = tensor(ctx, "warm", [P, 3])
        root = tensor(ctx, "root", [P, ROOT_STEPS + 1, 3 * NT])
        ssq_o = tensor(ctx, "ssq_o", [P, NT, 2])

        scope_a = ExitStack()
        q_t = tensor(scope_a, "q_t", [P, 2, GROUPS, T])
        k_t = tensor(scope_a, "k_t", [P, 2, GROUPS, T])
        v_n = tensor(scope_a, "v_n", [P, 2, GROUPS, NT, P])
        v_t = tensor(scope_a, "v_t", [P, 2, T])
        probs = tensor(scope_a, "probs", [P, 2, 2, NT, HALF])
        p_t = tensor(scope_a, "p_t", [P, PT_RING, T])
        ada_raw = tensor(scope_a, "ada_raw", [P, KT // 2, T])
        o_a = tensor(scope_a, "o_a", [P, T])
        o_sum = tensor(scope_a, "o_sum", [P, T])
        oh = tensor(scope_a, "oh", [P, PAIRS, T], F32R)
        ol = tensor(scope_a, "ol", [P, PAIRS, T], F32R)
        hh = tensor(scope_a, "hh", [P, KT, T], F32R)
        hl = tensor(scope_a, "hl", [P, KT, T], F32R)
        scope_a.close()
        scope_s = ExitStack()
        ada1 = tensor(scope_s, "ada1", [P, 2, KT, D // 2])
        acc1 = tensor(scope_s, "acc1", [P, MOD1 * P])
        x_nat = tensor(scope_s, "x_nat", [P, NT, D])
        xr_nat = tensor(scope_s, "xr_nat", [P, NT, D])
        xr = tensor(scope_s, "xr", [P, KT, T])
        rows_a = tensor(scope_s, "rows_a", [ROWS_A, P])
        rows_b = tensor(scope_s, "rows_b", [ROWS_B, P])
        xn = tensor(scope_s, "xn", [P, 2, T])
        other = tensor(scope_s, "other", [P, P])
        same = tensor(scope_s, "same", [4, P])
        scope_s.close()
        scope_f = ExitStack()
        sq2 = tensor(scope_f, "sq2", [P, 2, T])
        sq_sum = tensor(scope_f, "sq_sum", [P, T])
        diag = tensor(scope_f, "diag", [P, T])
        xn2 = tensor(scope_f, "xn2", [P, 4, HALF])
        xs2 = tensor(scope_f, "xs2", [P, 2, HALF])
        fh = tensor(scope_f, "fh", [P, KT, T], F32R)
        fl = tensor(scope_f, "fl", [P, KT, T], F32R)
        act_h = tensor(scope_f, "act_h", [P, FT, T], F32R)
        act_l = tensor(scope_f, "act_l", [P, FT, T], F32R)
        gate_in = tensor(scope_f, "gate_in", [P, T])
        gate = tensor(scope_f, "gate", [P, T])
        scope_f.close()
        scope_g = ExitStack()
        tensor(scope_g, "below_act_h", [P, (2 + 1 + 1 + 2 + 1 + 2 * KT) * T])
        wh_first = tensor(scope_g, "wh_first", [P, 2, KT, P], F32R)
        wl_first = tensor(scope_g, "wl_first", [P, 2, KT, P], F32R)
        scope_g.close()
        scope_e = ExitStack()
        out_n = tensor(scope_e, "out_n", [P, NT, D])
        nfin = tensor(scope_e, "nfin", [P, D])
        scope_e.close()

        banks = [ctx.enter_context(nc.psum_tensor(f"bank{i}", [P, T], F32)) for i in range(8)]
        proj, score, turn, o_acc = banks[0:2], banks[2:4], banks[4:6], banks[6:8]
        squares = banks[5]

        x_in = [sem(f"x_in{i}") for i in range(NT)]
        c_in, rows_in, nfin_in = sem("c_in"), sem("rows_in"), sem("nfin_in")
        ada1_in = [sem(f"ada1_in{i}") for i in range(len(ADA1) * KT // 2)]
        raw_in = [sem(f"raw_in{i}") for i in range(RING)]
        ada_in = sem("ada_in")
        const_done = sem("const_done")
        cond_step, mod_step = sem("cond_step"), sem("mod_step")
        acc1_step, weighted, pool_acc1_step = sem("acc1_step"), sem("weighted"), sem("pool_acc1_step")
        start_turned = sem("start_turned")
        start_taken = sem("start_taken")
        sq_done, sq_summed, sq_added = sem("sq_done"), sem("sq_summed"), sem("sq_added")
        row_squares = sem("row_squares")
        norm_step, root_done = sem("norm_step"), sem("root_done")
        low_done = [sem("low_done0"), sem("low_done1")]
        middle_xn, middle_low = sem("middle_xn"), sem("middle_low")
        pool_xr_done, shifted = sem("pool_xr_done"), sem("shifted")
        xr_done, diag_done, spread_done = sem("xr_done"), sem("diag_done"), sem("spread_done")
        xn_done = sem("xn_done")
        hh_done, hl_done = sem("hh_done"), sem("hl_done")
        mod1_done, mod1_taken = sem("mod1_done"), sem("mod1_taken")
        same_done = sem("same_done")
        h_ready, l_ready = sem("h_ready"), sem("l_ready")
        strip_done, strip_taken = sem("strip_done"), sem("strip_taken")
        tail_done = sem("tail_done")
        acc_step = sem("acc_step")
        y_done = sem("y_done")
        turned = [sem("turned0"), sem("turned1")]
        turn_taken = [sem("turn_taken0"), sem("turn_taken1")]
        scored, masked, nmax_done, exp_done = sem("scored"), sem("masked"), sem("nmax_done"), sem("exp_done")
        swapped, mix_dve, mix_act = sem("swapped"), sem("mix_dve"), sem("mix_act")
        scaled, pv_done = sem("scaled"), sem("pv_done")
        oa_copied, o_summed, oh_done, ol_done = sem("oa_copied"), sem("o_summed"), sem("oh_done"), sem("ol_done")
        x1_done = sem("x1_done")
        scores_seen, strip_seen = sem("scores_seen"), sem("strip_seen")
        fraw_in = [sem(f"fraw_in{i}") for i in range(FRAW)]
        fh_ready, fl_ready, fstrip_done = sem("fh_ready"), sem("fl_ready"), sem("fstrip_done")
        tap2_done, tap1_done, tap0_done = sem("tap2_done"), sem("tap1_done"), sem("tap0_done")
        gate_done, gated, act_h_done, act_l_done = sem("gate_done"), sem("gated"), sem("act_h_done"), sem("act_l_done")
        x2_done, nat_done, ssq_done, rstd_step, out_done, root_o_done, stored = (
            sem("x2_done"), sem("nat_done"), sem("ssq_done"), sem("rstd_step"), sem("out_done"),
            sem("root_o_done"), sem("stored"))
        out_pool_done = sem("out_pool_done")
        gained, out_a_done = sem("gained"), sem("out_a_done")

        block = ctx.enter_context(nc.Block())

        def turns_before(n):
            return 0 if isinstance(n, int) and n == 0 else 6 * n - 4

        SCORE_AT = {0: 0, 2: 1, 4: 2, 6: 3}
        TURN_V_AT = {3: 0, 5: 1, 7: 2}
        ADA_READ_AT = {0: 0, 1: 1, 2: 2, 3: 3, 5: 4, 6: 5, 7: 6, 8: 7}
        ADA_AT = 10
        TURN_P_AT = {12: 0, 14: 1, 15: 2, 16: 3}
        PV_AT = {14: 0, 15: 1, 16: 2, 17: 3}
        HALVES = 2 * STRIPS
        TURN_V_FIRST = {6: 0, 7: 1, 8: 2}
        ADA_READ_FIRST = {4: 0, 5: 1, 6: 2, 7: 3, 12: 4, 13: 5, 14: 6, 15: 7}
        ADA_FIRST = 17
        FILL_AT = {1: 3, 3: 3, 5: 3, 7: 10, 12: 3, 14: 1, 15: 1, 17: 4}
        OUT_AHEAD = 4
        out_banks = banks[0:OUT_AHEAD]
        fill_steps = [(o, t) for o in range(OUT_AHEAD) for t in range(KT - 1)]
        X1_STEPS = ([(o, slice(0, T)) for o in range(OUT_AHEAD)] +
                    [(o, slice(HALF * hf, HALF * (hf + 1))) for hf in range(2) for o in range(OUT_AHEAD, OUT_STRIPS)])

        def start_bank(c):
            return banks[(5, 6, 7, 4)[c]]

        BACK_AT = {4: (0,), 5: (1,), 6: (2, 3), 7: (4, 5, 6, 7)}

        def out_part(t, m):
            return t[:, m % 4, T * (m // 4):T * (m // 4 + 1)]

        def outer_before(t):
            return t if t < MIDDLE[1] else t - (MIDDLE[1] - MIDDLE[0])

        def low_of(t):
            if MIDDLE[0] <= t < MIDDLE[1]:
                return middle_low, t - MIDDLE[0] + 1
            return hl_done, outer_before(t) + 1

        def y_bank(o):
            return banks[(o + 4) % 8]

        def is_first(n):
            return isinstance(n, int) and n == 0

        def is_last(n):
            return isinstance(n, int) and n == PAIRS - 1

        def qkv_bank(n, par, s):
            return banks[s] if is_first(n) and s in (2, 3) else proj[(par + s) % 2]

        def qkv_slot(n, s):
            return RING if is_first(n) and s == RING else s % RING

        def split_at(n, h):
            if h % 2:
                return None
            if is_first(n) and h < 8:
                return h // 2 + 3 if h < 6 else None
            return h // 2 + 2

        def out_slot(o):
            return {2: 3, 3: 2}.get(o, o % FRING)

        def ada1_slice(c, t):
            if c < 2:
                return ada1[:, c, t]
            return (x_nat, xr_nat)[c - 2][:, t // 2, D // 2 * (t % 2):D // 2 * (t % 2 + 1)]

        def of_tiles(t, lo, hi):
            return t[:, 0:MOD1].rearrange("p (g t) -> p g t", g=2)[:, :, lo:hi]

        def columns(eng, at, n):
            return slice(at, at + n) if isinstance(at, int) else bass.ds(at, n)

        def bodies(eng, body):
            body(0, 0, True, False)
            with eng.Fori(0, (PAIRS - 2) // 2) as m:
                body(2 * m + 1, 1, True, True)
                body(2 * m + 2, 0, True, True)
            body(PAIRS - 1, 1, True, True)
            body(PAIRS, 0, False, True)

        def p_blocks(j):
            tiles = (2 * (j % 2), 2 * (j % 2) + 1)
            return [(b, part) for b in tiles for part in range(2) if not (j == 0 and b == 0 and part == 0)]

        def tile_of(t, f):
            at = slice(f, f + 1) if isinstance(f, int) else bass.ds(f, 1)
            return t[:, at].rearrange("p a n -> p (a n)")

        def tap(k, f):
            return cols_b[:, FT * k + f:FT * k + f + 1] if isinstance(f, int) else cols_b[:, bass.ds(FT * k + f, 1)]

        def split_slot(split, j, u, value, ready, dst):
            slot = u % FRING
            if dst is wh:
                if isinstance(j, int) and j < FRING:
                    free = (tail_done, FRING + j + 1)
                else:
                    free = (fstrip_done, j - FRING + 1)
                split(fraw_in[u % FRAW], value, raw[:, u % FRAW], wh[:, slot], free, ready)
            else:
                split(fh_ready, j + 1, raw[:, u % FRAW], wh[:, slot], wl[:, slot], ready)

        def split_ffn(split, i, u, ready, dst):
            split_slot(split, 4 * i + u + 3, (u + 3) % FRING, 16 * (2 * i + (u + 3) // 2 + 1), ready, dst)

        def split_down(split, k, u, pair, ready, dst):
            split_slot(split, UP_STRIPS + k + 3, (u + 3) % FRING, 16 * (UP_STRIPS // 2 + pair + 2 + u % 2), ready, dst)

        def split_out(split, o, ready, dst):
            g = QKV_STRIPS + o
            if dst is wh:
                last = {2: None, 3: QKV_STRIPS, 6: QKV_STRIPS + 4, 7: QKV_STRIPS + 3}.get(o, g - FRING + 1)
                split(raw_in[g % RING], 16 * (g // RING + 1), raw[:, g % RING], wh[:, out_slot(o)],
                      last and (strip_done, last), ready)
            else:
                split(h_ready, g + 1, raw[:, g % RING], wh[:, out_slot(o)], wl[:, out_slot(o)], ready)

        def split_first(split, j, ready, dst):
            if dst is wh:
                split(fraw_in[j], 16, raw[:, j], wh_first[:, j], (strip_done, QKV_STRIPS + OUT_AHEAD), ready)
            else:
                split(fh_ready, j + 1, raw[:, j], wh_first[:, j], wl_first[:, j], ready)

        def downs(eng, down):
            down(0, 0, 0)
            down(1, 1, 0)
            with eng.Fori(0, (FT - 6) // 4) as m:
                for u in range(4):
                    down(4 * m + 2 + u, (2 + u) % FRING, 2 * m + 1 + u // 2)
            for k in range(FT - 4, FT):
                down(k, k % FRING, k // 2)

        @block.sync
        def _(sp):
            sp.dma_start(cond[:, 0, :], c_cols).then_inc(c_in, 16)
            for i in range(NT):
                sp.dma_start(x_nat[:, i, :], x_rows[i]).then_inc(x_in[i], 16)
            ada1_src = ada[:, :, 0:MOD1 * P].rearrange("p t (g n) -> p t g n", g=2)

            def load_ada1(c):
                lo, hi = ADA1[c]
                for t in range(KT):
                    if c == 2:
                        sp.wait_ge(xr_done, 2)
                        sp.wait_ge(pool_xr_done, 2)
                        sp.wait_ge(start_turned, KT)
                    if c == 3:
                        sp.wait_ge(start_turned, 2 * KT + 1)
                    sp.dma_start(ada1_slice(c, t).rearrange("p (g n) -> p g n", g=2), ada1_src[:, t, :, P * lo:P * hi]
                                 ).then_inc(ada1_in[4 * c + t // 2], 16)

            def load_first(s):
                sp.dma_start(raw[:, s], w_qkv[:, :, 2 * GROUPS * D + s * D:2 * GROUPS * D + s * D + P]
                             ).then_inc(raw_in[s], 16)
            load_ada1(0)
            load_first(0)
            load_first(1)
            load_ada1(1)
            load_first(2)
            load_ada1(2)
            load_ada1(3)

            def load_strips(n, first):
                for s in range(RING if first else 0, STRIPS):
                    kind, g = strip_of(s)
                    at = {"q": 0, "k": 1, "v": 2}[kind] * GROUPS * D + g * D
                    src = w_qkv[:, :, columns(sp, at + P * n, P)]
                    ada_loads = (4, 7) if first else (2, 5)
                    if s in ada_loads:
                        half = ada_loads.index(s)
                        src_ada = ada[:, half * KT // 2:(half + 1) * KT // 2, columns(sp, MOD1 * P + T * n, T)]
                    sp.wait_ge(h_ready, STRIPS * n + s - RING + 1)
                    sp.wait_ge(l_ready, STRIPS * n + s - RING + 1)
                    if at == 0:
                        sp.sem_inc(strip_seen, 1)
                    sp.dma_start(raw[:, s % RING], src).then_inc(raw_in[s % RING], 16)
                    if s in ada_loads:
                        if not (first and half == 0):
                            sp.wait_ge(acc_step, KT * n + 4 * half)
                        elif first:
                            sp.wait_ge(*low_of(KT - 1))
                        sp.dma_start(ada_raw[:], src_ada).then_inc(ada_in, 16)
            load_strips(0, True)
            with sp.Fori(1, PAIRS) as n:
                load_strips(n, False)
            for o in range(OUT_STRIPS):
                g = QKV_STRIPS + o
                sp.wait_ge(h_ready, g - RING + 1)
                sp.wait_ge(l_ready, g - RING + 1)
                sp.dma_start(raw[:, g % RING], w_o[:, :, P * o:P * (o + 1)]).then_inc(raw_in[g % RING], 16)

            def up_columns(f, u):
                return w_up[:, :, columns(sp, FF * u + P * f, P)]
            for j in range(FRAW):
                sp.wait_ge(h_ready, QKV_STRIPS + OUT_STRIPS - 1 + j)
                sp.wait_ge(l_ready, QKV_STRIPS + OUT_STRIPS - 1 + j)
                sp.dma_start(raw[:, j], up_columns(0, j)).then_inc(fraw_in[j], 16)
            with sp.Fori(1, FT) as f:
                for u in range(2):
                    src = up_columns(f, u)
                    sp.wait_ge(fh_ready, 2 * f + u - FRAW + 1)
                    sp.wait_ge(fl_ready, 2 * f + u - FRAW + 1)
                    sp.dma_start(raw[:, u], src).then_inc(fraw_in[u], 16)
            with sp.Fori(0, FT // 2) as m:
                for u in range(2):
                    j = UP_STRIPS + 2 * m + u
                    src = w_down[columns(sp, 2 * m + u, 1)].rearrange("a p n -> p (a n)")
                    sp.wait_ge(fh_ready, j - FRAW + 1)
                    sp.wait_ge(fl_ready, j - FRAW + 1)
                    sp.dma_start(raw[:, u].rearrange("p t n -> p (t n)"), src).then_inc(fraw_in[u], 16)
            sp.wait_ge(act_l_done, FT)
            sp.wait_ge(fstrip_done, UP_STRIPS)
            sp.dma_start(nfin[:], norm_final.partition_broadcast(P)).then_inc(nfin_in, 16)
            for i in range(NT):
                for m, done, value in ((i + NT, out_done, i + 1), (i, (out_pool_done, out_a_done)[i // 2], i % 2 + 1)):
                    sp.wait_ge(done, value)
                    sp.dma_start(out_rows[i][:, T * (m // 4):T * (m // 4 + 1)], out_part(out_n, m)).then_inc(stored, 16)
            sp.wait_ge(stored, 16 * 2 * NT)

        @block.gpsimd
        def _(pool):
            nc.gpsimd.memset(ident[:], 0.0).then_inc(const_done, 1)
            nc.gpsimd.memset(ones[:], 1.0).then_inc(const_done, 1)
            nc.gpsimd.memset(mask[:], 0.0).then_inc(const_done, 1)
            nc.gpsimd.memset(same[:], 0.0).then_inc(const_done, 1)
            pool.wait_ge(const_done, 4)
            nc.gpsimd.affine_select(out=ident[:], in_=ident[:], compare_op=ALU.not_equal, fill=1.0, base=0,
                                    pattern=[[-1, P]], channel_multiplier=1).then_inc(const_done, 1)
            view = same[:].rearrange("p (a i) -> p a i", i=4)
            nc.gpsimd.affine_select(out=view, in_=view, compare_op=ALU.not_equal, fill=1.0, base=0,
                                    pattern=[[0, P // 4], [-1, 4]], channel_multiplier=1).then_inc(const_done, 1)
            pool.wait_ge(const_done, 6)
            for r in range(4):
                if r:
                    pool.wait_ge(const_done, 6 + 2 * r)
                part = mask[QUAD * r:QUAD * (r + 1), 0]
                nc.gpsimd.affine_select(out=part[:, 0:P], in_=part[:, 0:P], compare_op=ALU.is_ge, fill=MASKED,
                                        base=-r, pattern=[[1, P]], channel_multiplier=-4).then_inc(const_done, 1)
                nc.gpsimd.affine_select(out=part[:, P:HALF], in_=part[:, P:HALF], compare_op=ALU.is_ge, fill=MASKED,
                                        base=r, pattern=[[-1, P]], channel_multiplier=4).then_inc(const_done, 1)
            pool.wait_ge(const_done, 14)
            for g in range(2):
                part = mask[:, 1, P * g:P * (g + 1)]
                nc.gpsimd.affine_select(out=part, in_=part, compare_op=ALU.is_ge, fill=MASKED,
                                        base=0, pattern=[[-1, P]], channel_multiplier=1).then_inc(const_done, 1)
            pool.wait_ge(norm_step, ROOT_STEPS)
            for i in (2, 3):
                nc.gpsimd.tensor_scalar(xr_nat[:, i], x_nat[:, i], root[:, ROOT_STEPS, i:i + 1], 0.0, ALU.mult, ALU.add
                                        ).then_inc(pool_xr_done, 1)
            part = acc1[:, 2 * P * ADA1[1][0]:2 * P * ADA1[1][1]]
            for t in range(1, KT):
                pool.wait_ge(weighted, t + 1)
                if t >= 2:
                    pool.wait_ge(pool_acc1_step, t - 1)
                nc.gpsimd.tensor_tensor(part, ada1_slice(1, 0) if t == 1 else part, ada1_slice(1, t), ALU.add
                                        ).then_inc(pool_acc1_step, 1)
            for t in range(*MIDDLE):
                pool.wait_ge(middle_xn, t - MIDDLE[0] + 1)
                nc.gpsimd.tensor_tensor(hl[:, t], xn[:, t % 2], hh[:, t].bitcast(F32), ALU.subtract
                                        ).then_inc(middle_low, 1)
            for hf in range(2):
                for t in range(0, KT, 2):
                    tokens = slice(HALF * hf, HALF * (hf + 1))
                    pool.wait_ge(shifted, (KT * hf + t) // 2 + 1)
                    nc.gpsimd.tensor_tensor(fl[:, t, tokens], xs2[:, t // 2 % 2], fh[:, t, tokens].bitcast(F32),
                                            ALU.subtract).then_inc(low_done[0], 1)
            pool.wait_ge(gained, 2)
            pool.wait_ge(rstd_step, 3)
            for i in (0, 1):
                nc.gpsimd.tensor_scalar(out_part(out_n, i), out_part(out_n, i),
                                        root[:, ROOT_STEPS, 2 * NT + i:2 * NT + i + 1], 0.0, ALU.mult, ALU.add
                                        ).then_inc(out_pool_done, 1)

        @block.tensor
        def _(pe):
            pe.wait_ge(const_done, 16)
            for i in range(NT):
                pe.wait_ge(x_in[i], 16)
            for t in range(KT):
                if t >= 4:
                    pe.wait_ge(start_taken, t - 3)
                for i in range(NT):
                    last = nc.tensor.transpose(banks[t % 4][:, P * i:P * (i + 1)], x_nat[:, i, P * t:P * (t + 1)], ident[:])
                last.then_inc(start_turned, 1)
            pe.wait_ge(rows_in, 5 * 16)
            nc.tensor.transpose(banks[4][:, 0:ROWS_A], rows_a[:], ident[0:ROWS_A, 0:ROWS_A])
            nc.tensor.transpose(banks[4][:, P:P + ROWS_B], rows_b[:], ident[0:ROWS_B, 0:ROWS_B]).then_inc(start_turned, 1)
            nc.tensor.matmul(banks[7][:, 0:P], same[:], same[:], start=True, stop=True).then_inc(same_done, 1)

            pe.wait_ge(xr_done, 2)
            pe.wait_ge(pool_xr_done, 2)
            for t in range(KT):
                pe.wait_ge(start_taken, KT + 2 + t - 3 if t >= 4 else KT - 3 + t)
                for i in range(NT):
                    last = nc.tensor.transpose(banks[t % 4][:, P * i:P * (i + 1)], xr_nat[:, i, P * t:P * (t + 1)], ident[:])
                last.then_inc(start_turned, 1)

            def start_modulation(c):
                lo, hi = ADA1[c]
                if c == 1:
                    pe.wait_ge(pool_acc1_step, KT - 1)
                else:
                    pe.wait_ge(acc1_step, KT * max(c, 1))
                for i in range(2 * (hi - lo)):
                    at = P * (2 * lo + i)
                    last = nc.tensor.transpose(start_bank(c)[:, P * i:P * (i + 1)], acc1[:, at:at + P],
                                               ident[:])
                last.then_inc(mod1_done, 1)

            def start_strips(tiles):
                for s, t in [(s, t) for t in tiles for s in range(RING)]:
                    if t == 0:
                        pe.wait_ge(l_ready, s + 1)
                    if s == 0:
                        pe.wait_ge(*low_of(t))
                    bank = qkv_bank(0, 0, s)
                    if t == 0:
                        pe.wait_ge(start_taken, 2 * KT + 2)
                    nc.tensor.matmul(bank[:], wl[:, s, t], hh[:, t], start=(t == 0), stop=False)
                    nc.tensor.matmul(bank[:], wh[:, s, t], hh[:, t], start=False, stop=False)
                    last = nc.tensor.matmul(bank[:], wh[:, s, t], hl[:, t], start=False, stop=(t == KT - 1))
                    if t == KT - 1:
                        last.then_inc(strip_done, 1)
            start_modulation(0)
            start_strips((0, 1))
            start_modulation(1)
            start_modulation(2)
            start_strips((2, 3))
            start_modulation(3)
            start_strips((4, 5, 6, 7))

            def half_strip(bank, slot, half, xh, xl):
                for t in range(half * KT // 2, (half + 1) * KT // 2):
                    nc.tensor.matmul(bank[:], wl[:, slot, t], xh[:, t], start=(t == 0), stop=False)
                    nc.tensor.matmul(bank[:], wh[:, slot, t], xh[:, t], start=False, stop=False)
                    last = nc.tensor.matmul(bank[:], wh[:, slot, t], xl[:, t], start=False, stop=(t == KT - 1))
                return last

            def make_scores(n, par, d):
                if d == 0:
                    pe.wait_ge(strip_taken, STRIPS * n)
                pe.wait_ge(masked, 4 * (n - 1) + d + 1)
                side, tiles = d // 2, (2 * (d % 2), 2 * (d % 2) + 1)
                for b in tiles:
                    at = HALF * (b % 2)
                    if side == 0:
                        lo = P * max(b - 1, 0)
                        for hd in range(2):
                            e = slice(E * hd, E * (hd + 1))
                            last = nc.tensor.matmul(score[hd][:, at + (P if b == 0 else 0):at + HALF],
                                                    q_t[e, par, 0, P * b:P * (b + 1)],
                                                    k_t[e, par, 0, lo:P * (b + 1)], start=True, stop=True)
                    else:
                        for g in (1, 2):
                            for hd in range(2):
                                e = slice(E * hd, E * (hd + 1))
                                last = nc.tensor.matmul(score[hd][:, at + P * (g - 1):at + P * g],
                                                        q_t[e, par, g, P * b:P * (b + 1)],
                                                        k_t[e, par, g, P * b:P * (b + 1)], start=True, stop=True)
                last.then_inc(scored, 1)

            def turn_values(n, par, g):
                k, use = g % 2, g // 2
                pe.wait_ge(strip_taken, STRIPS * n + g + 1)
                if not (isinstance(n, int) and n == 0 and use == 0):
                    pe.wait_ge(turn_taken[k], turns_before(n) + use)
                src = v_t[:, (par + g) % 2]
                for b in range(NT):
                    keys = src[:, P * b:P * (b + 1)] if g == 0 else src[:, b:T:4]
                    last = nc.tensor.transpose(turn[k][:, P * b:P * (b + 1)], keys, ident[:])
                last.then_inc(turned[k], 1)

            def sum_ada(n):
                pe.wait_ge(acc_step, KT * (n + 1))
                pe.wait_ge(turn_taken[1], turns_before(n) + 1)
                for j in range(NT):
                    last = nc.tensor.transpose(turn[1][:, P * j:P * (j + 1)], acc[:, P * j:P * (j + 1)], ident[:])
                last.then_inc(turned[1], 1)

            def turn_probs(n, u, before):
                hd, j, k = u % 2, u // 2, u % 2
                pe.wait_ge(scaled, 8 * (n - 1) + u + 1)
                pe.wait_ge(turn_taken[k], turns_before(n) + before + j)
                for i, (b, part) in enumerate(p_blocks(j)):
                    last = nc.tensor.transpose(turn[k][:, P * i:P * (i + 1)],
                                               probs[:, hd, j // 2, b, P * part:P * (part + 1)], ident[:])
                last.then_inc(turned[k], 1)

            def weigh_values(n, par, u, before):
                hd, j, k = u % 2, u // 2, u % 2
                e = slice(E * hd, E * (hd + 1))
                pe.wait_ge(turn_taken[k], turns_before(n) + before + j + 1)
                if u == 0:
                    pe.wait_ge(o_summed, n)
                side = j // 2
                blocks = p_blocks(j)
                for i, (b, part) in enumerate(blocks):
                    if side == 0:
                        values = v_n[:, par, 0, b - 1 + part, e]
                    else:
                        values = v_n[:, par, 1 + part, b, e]
                    first = i == 0 or blocks[i - 1][0] != b
                    final = i == len(blocks) - 1 or blocks[i + 1][0] != b
                    last = nc.tensor.matmul(o_acc[side][e, P * b:P * (b + 1)], values, p_t[:, u % PT_RING, P * i:P * (i + 1)],
                                            start=first, stop=final)
                last.then_inc(pv_done, 1)

            def out_tiles(o, tiles, tokens=slice(0, T)):
                bank, slot = out_banks[o % 4], out_slot(o)
                for t in tiles:
                    nc.tensor.matmul(bank[:, tokens], wl[:, slot, t], oh[:, t, tokens], start=(t == 0), stop=False)
                    nc.tensor.matmul(bank[:, tokens], wh[:, slot, t], oh[:, t, tokens], start=False, stop=False)
                    last = nc.tensor.matmul(bank[:, tokens], wh[:, slot, t], ol[:, t, tokens], start=False,
                                            stop=(t == KT - 1))
                return last

            def sum_squares(hf):
                pe.wait_ge(sq_added, OUT_STRIPS - 1 + (OUT_STRIPS - OUT_AHEAD) * hf)
                for i in (2 * hf, 2 * hf + 1):
                    last = nc.tensor.matmul(squares[:, i:i + 1], sq_sum[:, P * i:P * (i + 1)], ones[:, 0:1],
                                            start=True, stop=True)
                last.then_inc(sq_summed, 1)

            def spread_root(hf):
                pe.wait_ge(diag_done, 2 * (hf + 1))
                nc.tensor.matmul(o_acc[hf][:, 0:HALF], ones[:], diag[:, HALF * hf:HALF * (hf + 1)],
                                 start=True, stop=True).then_inc(spread_done, 1)

            def begin_out(steps):
                for o, t in steps:
                    if t == 0:
                        pe.wait_ge(l_ready, QKV_STRIPS + o + 1)
                        if o < 2:
                            pe.wait_ge(strip_taken, QKV_STRIPS - 1 + o)
                        else:
                            pe.wait_ge(masked, 4 * PAIRS + 1)
                    if o == 0:
                        pe.wait_ge(ol_done, t + 1)
                    out_tiles(o, (t,))

            def body(n, par, project, attend):
                before = 2 if project else 0
                filled = 0
                for h in range(2 * RING if is_first(n) else 0, HALVES):
                    s = h // 2
                    if project:
                        g = STRIPS * n + s
                        if h % 2 == 0:
                            pe.wait_ge(l_ready, g + 1)
                            if not (is_first(n) and s == RING):
                                pe.wait_ge(strip_taken, g - 1)
                        last = half_strip(qkv_bank(n, par, s), qkv_slot(n, s), h % 2, hh, hl)
                        if h % 2 == 1:
                            last.then_inc(strip_done, 1)
                        turn_v_at = TURN_V_FIRST if is_first(n) else TURN_V_AT
                        if h in turn_v_at:
                            turn_values(n, par, turn_v_at[h])
                        if h == (ADA_FIRST if is_first(n) else ADA_AT):
                            sum_ada(n)
                    if attend:
                        if h in SCORE_AT:
                            make_scores(n, 1 - par, SCORE_AT[h])
                        if h in PV_AT:
                            for u in (2 * PV_AT[h], 2 * PV_AT[h] + 1):
                                weigh_values(n, 1 - par, u, before)
                        if h in TURN_P_AT:
                            for u in (2 * TURN_P_AT[h], 2 * TURN_P_AT[h] + 1):
                                turn_probs(n, u, before)
                    if attend and not project and h in FILL_AT:
                        begin_out(fill_steps[filled:filled + FILL_AT[h]])
                        filled += FILL_AT[h]
            bodies(pe, body)

            pe.wait_ge(ol_done, PAIRS)
            for o in range(OUT_AHEAD):
                out_tiles(o, (KT - 1,)).then_inc(strip_done, 1)
            for hf in range(2):
                tokens = slice(HALF * hf, HALF * (hf + 1))
                for o in range(OUT_AHEAD, OUT_STRIPS):
                    if hf == 0:
                        pe.wait_ge(l_ready, QKV_STRIPS + o + 1)
                    pe.wait_ge(x1_done, o - OUT_AHEAD + 1 if hf == 0 else o + 1)
                    out_tiles(o, range(KT), tokens).then_inc(tail_done, 1)
                    if hf == 1 and o == OUT_AHEAD:
                        sum_squares(0)
                    if hf == 1 and o == OUT_AHEAD + 1:
                        spread_root(0)

            pe.wait_ge(fl_ready, 2)
            for hf in range(2):
                tokens = slice(HALF * hf, HALF * (hf + 1))
                for t in range(KT):
                    if hf == 0 and t == 3:
                        sum_squares(1)
                    if hf == 0 and t == 6:
                        spread_root(1)
                    pe.wait_ge(low_done[t % 2], (KT * hf + t) // 2 + 1)
                    for j in range(2):
                        nc.tensor.matmul(banks[j][:, tokens], wl_first[:, j, t], fh[:, t, tokens], start=(t == 0), stop=False)
                        nc.tensor.matmul(banks[j][:, tokens], wh_first[:, j, t], fh[:, t, tokens], start=False, stop=False)
                        last = nc.tensor.matmul(banks[j][:, tokens], wh_first[:, j, t], fl[:, t, tokens],
                                                start=False, stop=(t == KT - 1))
                        if hf == 1 and t == KT - 1:
                            last.then_inc(fstrip_done, 1)

            def up(i):
                for w in range(2):
                    for u in range(2):
                        j = 4 * i + 2 * w + u
                        f = 2 * i + w
                        if isinstance(j, int) and j < 2:
                            continue
                        pe.wait_ge(fl_ready, j + 1)
                        if u == 0 and not (isinstance(i, int) and i == 0):
                            pe.wait_ge(gated, f - 1)
                        bank, slot = banks[2 * w + u], 2 * w + u
                        for t in range(KT):
                            nc.tensor.matmul(bank[:], wl[:, slot, t], fh[:, t], start=(t == 0), stop=False)
                            nc.tensor.matmul(bank[:], wh[:, slot, t], fh[:, t], start=False, stop=False)
                            last = nc.tensor.matmul(bank[:], wh[:, slot, t], fl[:, t], start=False, stop=(t == KT - 1))
                        last.then_inc(fstrip_done, 1)
            up(0)
            with pe.Fori(1, FT // 2) as i:
                up(i)

            def down(k, u, pair):
                static = isinstance(k, int)
                if static and k >= FT - 2:
                    return
                slot = u
                pe.wait_ge(fl_ready, UP_STRIPS + k + 1)
                pe.wait_ge(act_l_done, k + 1)
                for o in range(KT):
                    if static and k == 0 and o in (4, 6):
                        pe.wait_ge(gated, FT - 1 + (o == 6))
                    start = static and k == 0
                    at = slice(k, k + 1) if static else bass.ds(k, 1)
                    xh = act_h[:, at].rearrange("p a n -> p (a n)")
                    xl = act_l[:, at].rearrange("p a n -> p (a n)")
                    y = y_bank(o)
                    nc.tensor.matmul(y[:], wl[:, slot, o], xh, start=start, stop=False)
                    nc.tensor.matmul(y[:], wh[:, slot, o], xh, start=False, stop=False)
                    last = nc.tensor.matmul(y[:], wh[:, slot, o], xl, start=False, stop=False)
                last.then_inc(fstrip_done, 1)
            downs(pe, down)

            pe.wait_ge(fl_ready, UP_STRIPS + FT)
            pe.wait_ge(act_l_done, FT)
            for o in range(KT):
                for k in (FT - 2, FT - 1):
                    slot = k % FRING
                    nc.tensor.matmul(y_bank(o)[:], wl[:, slot, o], act_h[:, k], start=False, stop=False)
                    nc.tensor.matmul(y_bank(o)[:], wh[:, slot, o], act_h[:, k], start=False, stop=False)
                    last = nc.tensor.matmul(y_bank(o)[:], wh[:, slot, o], act_l[:, k], start=False, stop=(k == FT - 1))
                last.then_inc(y_done, 1)
                for m in BACK_AT.get(o, ()):
                    pe.wait_ge(x2_done, 4 if m < 4 else KT if m < 6 else KT + 1)
                    for q in range(4):
                        last = nc.tensor.transpose(y_bank(m)[:, P * q:P * (q + 1)],
                                                   xT[:, 4 * (m // 4) + q, P * (m % 4):P * (m % 4 + 1)], ident[:])
                    last.then_inc(nat_done, 1)

        @block.scalar
        def _(act):
            act.dma_start(rows_a[0:MOD], b_ada[0].rearrange("(r p) -> r p", p=P)).then_inc(rows_in, 16)
            act.dma_start(rows_a[MOD:MOD + KT], norm_mix[0].rearrange("(r p) -> r p", p=P)).then_inc(rows_in, 16)
            act.dma_start(rows_a[MOD + KT:ROWS_A], norm_ffn[0].rearrange("(r p) -> r p", p=P)).then_inc(rows_in, 16)
            act.dma_start(rows_b[0:3 * FT], ffn_conv_w[0].rearrange("k (r p) -> (k r) p", p=P)).then_inc(rows_in, 16)
            act.dma_start(rows_b[3 * FT:ROWS_B], ffn_conv_b[0].rearrange("(r p) -> r p", p=P)).then_inc(rows_in, 16)
            act.wait_ge(c_in, 16)
            nc.scalar.activation(cond[:, 1], cond[:, 0], ACT.Exp, scale=-1.0).then_inc(cond_step, 1)

            for i in range(NT):
                act.wait_ge(x_in[i], 16)
                nc.scalar.activation(xr_nat[:, i], x_nat[:, i], ACT.Square, accum_out=root[:, 0, i:i + 1]
                                     ).then_inc(row_squares, 1)
            act.wait_ge(const_done, 4)
            nc.scalar.activation(warm[:, 2:3], ones[:, 0:1], ACT.Sqrt)

            def root_of(q, lo, hi):
                act.wait_ge(norm_step, 1 if q == 0 else ROOT_STEPS + 2 * q - 1)
                nc.scalar.activation(root[:, 2, lo:hi], root[:, 1, lo:hi], ACT.Sqrt).then_inc(root_done, 1)
            root_of(0, 0, NT)
            for t in range(KT):
                act.wait_ge(start_turned, t + 1)
                nc.scalar.activation(xT[:, t], banks[t % 4][:], ACT.Copy).then_inc(start_taken, 1)
            act.wait_ge(start_turned, KT + 1)
            nc.scalar.activation(cols_a[:], banks[4][:, 0:ROWS_A], ACT.Copy).then_inc(start_taken, 1)
            nc.scalar.activation(cols_b[:], banks[4][:, P:P + ROWS_B], ACT.Copy).then_inc(start_taken, 1)
            for t in range(KT):
                act.wait_ge(start_turned, KT + 2 + t)
                nc.scalar.activation(xr[:, t], banks[t % 4][:], ACT.Copy).then_inc(start_taken, 1)

            def split_h(sem_in, value, src, dst, free, done):
                act.wait_ge(sem_in, value)
                if free is not None:
                    act.wait_ge(*free)
                nc.scalar.activation(dst, src, ACT.Copy).then_inc(done, 1)

            def split_qkv(n, s):
                g = STRIPS * n + s
                free = None if isinstance(g, int) and g <= RING else (strip_done, g - RING + 1)
                slot = qkv_slot(n, s)
                split_h(raw_in[s % RING], 16 * (GROUPS * n + s // RING + 1), raw[:, s % RING], wh[:, slot],
                        free, h_ready)

            def weigh_ada1(t):
                act.wait_ge(ada1_in[4 + t // 2], 32)
                for k in (t, t + 1):
                    nc.scalar.activation(ada1_slice(1, k), ada1_slice(1, k), ACT.Copy, scale=cond[:, 4, k:k + 1]
                                         ).then_inc(weighted, 1)

            def start_high(c):
                act.wait_ge(mod_step, 2 * (c + 1))
                for t in range(*ADA1[c]):
                    nc.scalar.activation(hh[:, t], xr[:, t], ACT.Identity, bias=mod[:, t:t + 1],
                                         scale=gain[:, 0, t:t + 1]).then_inc(hh_done, 1)
                    if t in range(*MIDDLE):
                        act.wait_ge(*low_of(t - 2))
                        nc.scalar.activation(xn[:, t % 2], xr[:, t], ACT.Identity, bias=mod[:, t:t + 1],
                                             scale=gain[:, 0, t:t + 1]).then_inc(middle_xn, 1)

            split_qkv(0, 0)
            split_qkv(0, 1)
            weigh_ada1(0)
            weigh_ada1(2)
            start_high(0)
            split_qkv(0, 2)
            weigh_ada1(4)
            weigh_ada1(6)
            for c in (1, 2, 3):
                start_high(c)

            def take_turn(n, use, dst):
                act.wait_ge(turned[1], turns_before(n) + use + 1)
                nc.scalar.activation(dst, turn[1][:], ACT.Copy).then_inc(turn_taken[1], 1)

            def body(n, par, project, attend):
                before = 2 if project else 0
                for h in range(HALVES):
                    s = h // 2
                    if project:
                        if split_at(n, h) is not None:
                            split_qkv(n, split_at(n, h))
                        if h % 2 == 1:
                            act.wait_ge(strip_done, STRIPS * n + s + 1)
                            kind, g = strip_of(s)
                            if is_first(n) and s == 2:
                                act.wait_ge(turned[0], 1)
                            dst = {"v": v_t[:, (par + g) % 2], "q": q_t[:, par, g], "k": k_t[:, par, g]}[kind]
                            src, dst = in_order(g, kind, qkv_bank(n, par, s)[:], dst)
                            nc.scalar.activation(dst, src, ACT.Copy).then_inc(strip_taken, 1)
                        if (TURN_V_FIRST if is_first(n) else TURN_V_AT).get(h) == 1:
                            take_turn(n, 0, v_n[:, par, 1].rearrange("p b e -> p (b e)"))
                    if attend and not project and h == 0:
                        split_out(split_h, 3, h_ready, wh)
                    if attend:
                        if h in SCORE_AT:
                            d = SCORE_AT[h]
                            act.wait_ge(nmax_done, 4 * (n - 1) + d + 1)
                            side = d // 2
                            for b in (2 * (d % 2), 2 * (d % 2) + 1):
                                for hd in range(2):
                                    tile = probs[:, hd, side, b, (P if d == 0 and b == 0 else 0):HALF]
                                    last = nc.scalar.activation(tile, tile, ACT.Exp, bias=nmax[:, side, b, hd:hd + 1],
                                                                scale=SCORE_SCALE, accum_out=stat[:, side, b, 1, hd:hd + 1])
                            last.then_inc(exp_done, 1)
                        if h == 8:
                            act.wait_ge(mix_dve, MIX_STEPS * (n - 1) + 3)
                            nc.scalar.activation(mix[:, 3:5], mix[:, 1:3], ACT.Exp, scale=SCORE_SCALE).then_inc(mix_act, 1)
                        if h in TURN_P_AT:
                            u = 2 * TURN_P_AT[h] + 1
                            take_turn(n, before + u // 2, p_t[:, u % PT_RING])
                    if is_last(n) and h == HALVES - 2:
                        split_out(split_h, 2, h_ready, wh)
                if attend:
                    act.wait_ge(pv_done, 8 * n)
                    nc.scalar.activation(o_a[:].rearrange("p (b j r) -> p b j r", b=NT, r=4),
                                         o_acc[0][:].rearrange("p (b r j) -> p b j r", b=NT, r=4),
                                         ACT.Copy).then_inc(oa_copied, 1)
                    act.wait_ge(o_summed, n + 1)
                    nc.scalar.activation(oh[:, bass.ds(n - 1, 1)].rearrange("p a n -> p (a n)"), o_sum[:],
                                         ACT.Copy).then_inc(oh_done, 1)
            bodies(act, body)

            nc.scalar.activation(warm[:, 0:1], ones[:, 0:1], ACT.Sqrt)

            def square(e):
                o, tokens = X1_STEPS[e]
                act.wait_ge(x1_done, e + 1)
                if e >= 3:
                    act.wait_ge(sq_added, e - 2)
                nc.scalar.activation(sq2[:, e % 2, tokens] if e else sq_sum[:], xT[:, o, tokens], ACT.Square
                                     ).then_inc(sq_done, 1)

            def high_part(hf, t):
                tokens = slice(HALF * hf, HALF * (hf + 1))
                n = KT * hf + t
                act.wait_ge(xn_done, outer_before(KT) + n + 1)
                shift = mod[:, 3 * KT + t:3 * KT + t + 1]
                nc.scalar.activation(fh[:, t, tokens], xn2[:, t % 4], ACT.Identity, bias=shift).then_inc(hh_done, 1)
                if t % 2 == 0:
                    if n >= 4:
                        act.wait_ge(low_done[0], (n - 4) // 2 + 1)
                    nc.scalar.activation(xs2[:, t // 2 % 2], xn2[:, t % 4], ACT.Identity, bias=shift).then_inc(shifted, 1)

            for o in range(OUT_AHEAD):
                split_out(split_h, OUT_AHEAD + o, h_ready, wh)
                square(o)
            for e in range(4, 8):
                square(e)
                if e == 5:
                    split_first(split_h, 0, fh_ready, wh)
            root_of(1, NT, NT + 2)
            split_first(split_h, 1, fh_ready, wh)
            square(8)
            square(9)
            for t in range(3):
                high_part(0, t)
            square(10)
            high_part(0, 3)
            split_slot(split_h, 2, 2, 32, fh_ready, wh)
            square(11)
            high_part(0, 4)
            high_part(0, 5)
            root_of(2, NT + 2, 2 * NT)
            for t in range(6, KT):
                high_part(0, t)
            for t in range(KT):
                high_part(1, t)

            def gate_branch(f):
                act.wait_ge(tap0_done, f + 1)
                if not (isinstance(f, int) and f == 0):
                    act.wait_ge(act_l_done, f)
                nc.scalar.activation(gate[:], gate_in[:], ACT.Silu).then_inc(gate_done, 1)
                act.wait_ge(gated, f + 1)
                nc.scalar.activation(tile_of(act_h, f), gate[:], ACT.Copy).then_inc(act_h_done, 1)

            def up(i):
                for w in range(2):
                    f = 2 * i + w
                    for u in range(2):
                        j = 4 * i + 2 * w + u
                        split_ffn(split_h, i, 2 * w + u, fh_ready, wh)
                        if u == 0 and not (isinstance(f, int) and f == 0):
                            gate_branch(f - 1)
                        if u == 1:
                            act.wait_ge(fstrip_done, j)
                            nc.scalar.activation(gate_in[:], banks[2 * w][:], ACT.Identity, bias=tap(3, f),
                                                 scale=tap(2, f)).then_inc(tap2_done, 1)
            up(0)
            with act.Fori(1, FT // 2) as i:
                up(i)
            gate_branch(FT - 1)

            def down(k, u, pair):
                if not (isinstance(k, int) and k >= FT - 3):
                    split_down(split_h, k, u, pair, fh_ready, wh)
            downs(act, down)

            nc.scalar.activation(warm[:, 1:2], ones[:, 0:1], ACT.Sqrt)
            for m in range(2 * NT):
                act.wait_ge(nat_done, m + 1)
                nc.scalar.activation(out_part(out_n, m), y_bank(m)[:], ACT.Square,
                                     accum_out=ssq_o[:, m % 4, m // 4:m // 4 + 1]).then_inc(ssq_done, 1)
                if m in (5, 7):
                    pair = (m - 5) // 2
                    act.wait_ge(rstd_step, 2 + 3 * pair)
                    lo = 2 * NT + 2 * pair
                    nc.scalar.activation(root[:, 2, lo:lo + 2], root[:, 1, lo:lo + 2], ACT.Sqrt).then_inc(root_o_done, 1)
            for i in (2, 3):
                act.wait_ge(gained, NT)
                act.wait_ge(rstd_step, 6)
                nc.scalar.activation(out_part(out_n, i), out_part(out_n, i), ACT.Copy,
                                     scale=root[:, ROOT_STEPS, 2 * NT + i:2 * NT + i + 1]).then_inc(out_a_done, 1)

        @block.vector
        def _(dve):
            dve.wait_ge(cond_step, 1)
            nc.vector.tensor_scalar(cond[:, 2], cond[:, 1], 1.0, None, ALU.add).then_inc(cond_step, 1)
            dve.wait_ge(cond_step, 2)
            nc.vector.reciprocal(cond[:, 3], cond[:, 2]).then_inc(cond_step, 1)
            dve.wait_ge(cond_step, 3)
            nc.vector.tensor_tensor(cond[:, 4], cond[:, 0], cond[:, 3], ALU.mult).then_inc(cond_step, 1)
            dve.wait_ge(cond_step, 4)
            def accumulate(c, slices=range(KT)):
                lo, hi = ADA1[c]
                part = acc1[:, 2 * P * lo:2 * P * hi]
                for t in slices:
                    if t % 2 == 0:
                        dve.wait_ge(ada1_in[4 * c + t // 2], 32)
                    if t == 0:
                        nc.vector.tensor_scalar(part, ada1_slice(c, 0), cond[:, 4, 0:1], None, ALU.mult
                                                ).then_inc(acc1_step, 1)
                    else:
                        dve.wait_ge(acc1_step, KT * max(c - 1, 0) + t)
                        nc.vector.scalar_tensor_tensor(part, ada1_slice(c, t), cond[:, 4, t:t + 1], part,
                                                       ALU.mult, ALU.add).then_inc(acc1_step, 1)

            def add_square(e):
                tokens = X1_STEPS[e][1]
                dve.wait_ge(sq_done, e + 1)
                if e >= 2:
                    dve.wait_ge(sq_added, e - 1)
                nc.vector.tensor_tensor(sq_sum[:, tokens], sq_sum[:, tokens], sq2[:, e % 2, tokens], ALU.add
                                        ).then_inc(sq_added, 1)

            def first_root():
                v, y = root[:, 1, 0:NT], root[:, 3, 0:NT]
                nc.vector.tensor_scalar(v, root[:, 0, 0:NT], 1.0 / D, EPS, ALU.mult, ALU.add).then_inc(norm_step, 1)
                dve.wait_ge(root_done, 1)
                nc.vector.reciprocal(y, root[:, 2, 0:NT]).then_inc(norm_step, 1)
                dve.wait_ge(norm_step, 2)
                nc.vector.tensor_tensor(root[:, 4, 0:NT], y, y, ALU.mult).then_inc(norm_step, 1)
                dve.wait_ge(norm_step, 3)
                nc.vector.tensor_tensor(root[:, 5, 0:NT], root[:, 4, 0:NT], v, ALU.mult).then_inc(norm_step, 1)
                dve.wait_ge(norm_step, 4)
                nc.vector.tensor_scalar(root[:, 0, 0:NT], root[:, 5, 0:NT], -0.5, 1.5, ALU.mult, ALU.add
                                        ).then_inc(norm_step, 1)
                dve.wait_ge(norm_step, 5)
                nc.vector.tensor_tensor(root[:, ROOT_STEPS, 0:NT], y, root[:, 0, 0:NT], ALU.mult).then_inc(norm_step, 1)
                dve.wait_ge(norm_step, ROOT_STEPS)

            dve.wait_ge(row_squares, NT)
            first_root()

            for i in range(2):
                nc.vector.tensor_scalar(xr_nat[:, i], x_nat[:, i], root[:, ROOT_STEPS, i:i + 1], None, ALU.mult
                                        ).then_inc(xr_done, 1)
            def split_l(ready, value, src, high, dst, done):
                dve.wait_ge(ready, value)
                nc.vector.tensor_tensor(dst, src, high.bitcast(F32), ALU.subtract).then_inc(done, 1)

            def split_qkv(n, s):
                split_l(h_ready, STRIPS * n + s + 1, raw[:, s % RING], wh[:, qkv_slot(n, s)],
                        wl[:, qkv_slot(n, s)], l_ready)

            dve.sem_inc(masked, 1)
            dve.sem_inc(o_summed, 1)
            def start_gains(c):
                lo, hi = ADA1[c]
                dve.wait_ge(mod1_done, c + 1)
                nc.vector.tensor_reduce(of_tiles(mod_raw, lo, hi),
                                        start_bank(c)[:].rearrange("p (g t n) -> p g t n", g=2, n=P), AX.X, ALU.add
                                        ).then_inc(mod1_taken, 1)
                dve.wait_ge(mod1_taken, c + 1)
                dve.wait_ge(start_taken, KT + 2)
                nc.vector.tensor_tensor(of_tiles(mod, lo, hi), of_tiles(mod_raw, lo, hi), of_tiles(cols_a, lo, hi), ALU.add
                                        ).then_inc(mod_step, 1)
                dve.wait_ge(mod_step, 2 * c + 1)
                nc.vector.scalar_tensor_tensor(gain[:, 0, lo:hi], mod[:, KT + lo:KT + hi], 1.0,
                                               cols_a[:, MOD + lo:MOD + hi], ALU.add, ALU.mult).then_inc(mod_step, 1)
                dve.wait_ge(mod_step, 2 * (c + 1))

            def start_tiles(c):
                for t in range(*ADA1[c]):
                    dve.wait_ge(start_taken, KT + 2 + t + 1)
                    if t >= 2:
                        dve.wait_ge(*low_of(t - 2))
                    nc.vector.tensor_scalar(xn[:, t % 2], xr[:, t], gain[:, 0, t:t + 1], mod[:, t:t + 1],
                                            ALU.mult, ALU.add).then_inc(xn_done, 1)
                    dve.wait_ge(xn_done, outer_before(t) + 1)
                    dve.wait_ge(hh_done, t + 1)
                    nc.vector.tensor_tensor(hl[:, t], xn[:, t % 2], hh[:, t].bitcast(F32), ALU.subtract
                                            ).then_inc(hl_done, 1)

            accumulate(0)
            split_qkv(0, 0)
            start_gains(0)
            split_qkv(0, 1)
            start_tiles(0)
            dve.wait_ge(same_done, 1)
            dve.wait_ge(const_done, 16)
            nc.vector.tensor_scalar(other[:], banks[7][:, 0:P], 1.0, -MASKED, ALU.subtract, ALU.mult).then_inc(same_done, 1)
            dve.wait_ge(same_done, 2)
            nc.vector.tensor_tensor(mask[:, 1, P:HALF], mask[:, 1, P:HALF], other[:], ALU.min).then_inc(same_done, 1)
            dve.wait_ge(same_done, 3)
            split_qkv(0, 2)
            accumulate(2, range(0, 6))
            start_gains(1)
            accumulate(2, range(6, KT))
            start_gains(2)
            accumulate(3)
            start_gains(3)
            start_tiles(3)

            def take_turn(n, use, dst):
                dve.wait_ge(turned[0], turns_before(n) + use + 1)
                nc.vector.tensor_copy(dst, turn[0][:]).then_inc(turn_taken[0], 1)

            def mask_scores(n, d):
                dve.wait_ge(scored, 4 * (n - 1) + d + 1)
                dve.sem_inc(scores_seen, 1)
                side = d // 2
                for b in (2 * (d % 2), 2 * (d % 2) + 1):
                    lo = P if d == 0 and b == 0 else 0
                    for hd in range(2):
                        last = nc.vector.tensor_tensor_reduce(
                            probs[:, hd, side, b, lo:HALF], score[hd][:, HALF * (b % 2) + lo:HALF * (b % 2 + 1)],
                            mask[:, side, lo:HALF], 1.0, MASKED, ALU.add, ALU.max, stat[:, side, b, 0, hd:hd + 1])
                last.then_inc(masked, 1)
                dve.wait_ge(masked, 4 * (n - 1) + d + 2)
                b = 2 * (d % 2)
                nc.vector.tensor_scalar(nmax[:, side, b:b + 2], stat[:, side, b:b + 2, 0], -SCORE_SCALE, None,
                                        ALU.mult).then_inc(nmax_done, 1)

            def weigh(units):
                for u in units:
                    hd, j = u % 2, u // 2
                    side = j // 2
                    for b in (2 * (j % 2), 2 * (j % 2) + 1):
                        tile = probs[:, hd, side, b, (P if j == 0 and b == 0 else 0):HALF]
                        last = nc.vector.tensor_scalar(tile, tile, mix[:, 5, side, b, hd:hd + 1], None, ALU.mult)
                    last.then_inc(scaled, 1)

            def body(n, par, project, attend):
                before = 2 if project else 0
                for h in range(HALVES):
                    s = h // 2
                    if project:
                        if split_at(n, h) is not None:
                            split_qkv(n, split_at(n, h))
                        ada_read_at = ADA_READ_FIRST if is_first(n) else ADA_READ_AT
                        if h in ada_read_at:
                            t = ada_read_at[h]
                            if t % 4 == 0:
                                dve.wait_ge(ada_in, 16 * (2 * n + t // 4 + 1))
                            src = ada_raw[:, t % 4]
                            if t == 0:
                                ins = nc.vector.tensor_scalar(acc[:], src, cond[:, 4, 0:1], None, ALU.mult)
                            else:
                                dve.wait_ge(acc_step, KT * n + t)
                                ins = nc.vector.scalar_tensor_tensor(acc[:], src, cond[:, 4, t:t + 1], acc[:],
                                                                     ALU.mult, ALU.add)
                            ins.then_inc(acc_step, 1)
                        if h == (ADA_FIRST if is_first(n) else ADA_AT):
                            dve.wait_ge(turned[1], turns_before(n) + 2)
                            nc.vector.tensor_reduce(mod_raw[:, bass.ds(MOD1 + NT * n, NT)],
                                                    turn[1][:].rearrange("p (t n) -> p t n", n=P), AX.X, ALU.add
                                                    ).then_inc(turn_taken[1], 1)
                        g = (TURN_V_FIRST if is_first(n) else TURN_V_AT).get(h)
                        if g in (0, 2):
                            take_turn(n, g // 2, v_n[:, par, g].rearrange("p b e -> p (b e)"))
                    if attend:
                        if h in SCORE_AT:
                            mask_scores(n, SCORE_AT[h])
                        if h == 8:
                            dve.wait_ge(exp_done, 4 * n)
                            for a in range(4):
                                for b in range(4):
                                    last = nc.vector.tensor_copy(swap[QUAD * b:QUAD * (b + 1), :, a],
                                                                 stat[QUAD * a:QUAD * (a + 1), :, b])
                            last.then_inc(swapped, 1)
                            dve.wait_ge(swapped, n)
                            nc.vector.tensor_tensor(mix[:, 0], swap[:, ::-1, :, 0], stat[:, :, :, 0],
                                                    ALU.max).then_inc(mix_dve, 1)
                            dve.wait_ge(mix_dve, MIX_STEPS * (n - 1) + 1)
                            nc.vector.tensor_tensor(mix[:, 1], stat[:, :, :, 0], mix[:, 0], ALU.subtract).then_inc(mix_dve, 1)
                            nc.vector.tensor_tensor(mix[:, 2], swap[:, ::-1, :, 0], mix[:, 0],
                                                    ALU.subtract).then_inc(mix_dve, 1)
                        if h == 9:
                            dve.wait_ge(mix_act, n)
                            nc.vector.tensor_tensor(mix[:, 5], stat[:, :, :, 1], mix[:, 3], ALU.mult).then_inc(mix_dve, 1)
                            nc.vector.tensor_tensor(mix[:, 6], swap[:, ::-1, :, 1], mix[:, 4], ALU.mult).then_inc(mix_dve, 1)
                            dve.wait_ge(mix_dve, MIX_STEPS * (n - 1) + 5)
                            nc.vector.tensor_tensor(mix[:, 7], mix[:, 5], mix[:, 6], ALU.add).then_inc(mix_dve, 1)
                            dve.wait_ge(mix_dve, MIX_STEPS * (n - 1) + 6)
                            nc.vector.reciprocal(mix[:, 8], mix[:, 7]).then_inc(mix_dve, 1)
                            dve.wait_ge(mix_dve, MIX_STEPS * (n - 1) + 7)
                            nc.vector.tensor_tensor(mix[:, 5], mix[:, 3], mix[:, 8], ALU.mult).then_inc(mix_dve, 1)
                            dve.wait_ge(mix_dve, MIX_STEPS * n)
                            weigh(range(4))
                        if h in TURN_P_AT:
                            u = 2 * TURN_P_AT[h]
                            take_turn(n, before + u // 2, p_t[:, u % PT_RING])
                            if u == 0:
                                weigh(range(4, 8))
                    if is_last(n) and h == HALVES - 2:
                        split_out(split_l, 2, l_ready, wl)
                    if attend and not project and h == 0:
                        split_out(split_l, 3, l_ready, wl)
                if attend:
                    dve.wait_ge(oa_copied, n)
                    nat = "p (b j r) -> p b j r"
                    nc.vector.tensor_tensor(o_sum[:].rearrange(nat, b=NT, r=4), o_a[:].rearrange(nat, b=NT, r=4),
                                            o_acc[1][:].rearrange("p (r b j) -> p b j r", b=NT, r=4),
                                            ALU.add).then_inc(o_summed, 1)
                    dve.wait_ge(oh_done, n)
                    at = bass.ds(n - 1, 1)
                    nc.vector.tensor_tensor(ol[:, at].rearrange("p a n -> p (a n)"), o_sum[:],
                                            oh[:, at].rearrange("p a n -> p (a n)").bitcast(F32),
                                            ALU.subtract).then_inc(ol_done, 1)
            bodies(dve, body)

            dve.wait_ge(turn_taken[1], turns_before(PAIRS - 1) + 2)
            nc.vector.tensor_tensor(mod[:, MOD1:MOD], mod_raw[:, MOD1:MOD], cols_a[:, MOD1:MOD], ALU.add
                                    ).then_inc(mod_step, 1)
            dve.wait_ge(mod_step, 2 * len(ADA1) + 1)
            nc.vector.scalar_tensor_tensor(gain[:, 1], mod[:, 4 * KT:5 * KT], 1.0, cols_a[:, MOD + KT:MOD + 2 * KT],
                                           ALU.add, ALU.mult).then_inc(mod_step, 1)
            dve.wait_ge(mod_step, 2 * len(ADA1) + 2)

            def add_attention(e):
                o, tokens = X1_STEPS[e]
                if e < OUT_AHEAD:
                    dve.wait_ge(strip_done, QKV_STRIPS + o + 1)
                else:
                    dve.wait_ge(tail_done, e - OUT_AHEAD + 1)
                nc.vector.scalar_tensor_tensor(xT[:, o, tokens], out_banks[o % 4][:, tokens],
                                               mod[:, 2 * KT + o:2 * KT + o + 1], xT[:, o, tokens],
                                               ALU.mult, ALU.add).then_inc(x1_done, 1)
                if e not in (0, 1, 8):
                    add_square(e - 1)

            def second_mean(hf):
                lo = NT + 2 * hf
                dve.wait_ge(sq_summed, hf + 1)
                nc.vector.tensor_scalar(root[:, 1, lo:lo + 2], squares[:, 2 * hf:2 * hf + 2], 1.0 / D, EPS,
                                        ALU.mult, ALU.add).then_inc(norm_step, 1)

            def second_root(hf):
                lo = NT + 2 * hf
                dve.wait_ge(root_done, 2 + hf)
                nc.vector.reciprocal(root[:, ROOT_STEPS, lo:lo + 2], root[:, 2, lo:lo + 2]).then_inc(norm_step, 1)
                dve.wait_ge(norm_step, ROOT_STEPS + 2 * (hf + 1))
                for i in (2 * hf, 2 * hf + 1):
                    nc.vector.tensor_scalar(diag[:, P * i:P * (i + 1)], ident[:], root[:, ROOT_STEPS, NT + i:NT + i + 1],
                                            None, ALU.mult).then_inc(diag_done, 1)

            def second_norm(hf, t):
                tokens = slice(HALF * hf, HALF * (hf + 1))
                if t == 0:
                    dve.wait_ge(spread_done, hf + 1)
                n = KT * hf + t
                if n >= 4:
                    dve.wait_ge(low_done[1] if t % 2 else shifted, (n - 4) // 2 + 1)
                nc.vector.scalar_tensor_tensor(xn2[:, t % 4], xT[:, t, tokens], gain[:, 1, t:t + 1],
                                               o_acc[hf][:, 0:HALF], ALU.mult, ALU.mult).then_inc(xn_done, 1)

            def odd_low(hf, t):
                tokens = slice(HALF * hf, HALF * (hf + 1))
                dve.wait_ge(hh_done, KT * (hf + 1) + t + 1)
                nc.vector.scalar_tensor_tensor(fl[:, t, tokens], xn2[:, t % 4], mod[:, 3 * KT + t:3 * KT + t + 1],
                                               fh[:, t, tokens].bitcast(F32), ALU.add, ALU.subtract
                                               ).then_inc(low_done[1], 1)

            for o in range(OUT_AHEAD):
                add_attention(o)
                split_out(split_l, OUT_AHEAD + o, l_ready, wl)
            for e in range(4, 8):
                add_attention(e)
                if e == 5:
                    split_first(split_l, 0, fl_ready, wl)
            add_square(7)
            second_mean(0)
            second_root(0)
            split_first(split_l, 1, fl_ready, wl)
            add_attention(8)
            add_attention(9)
            second_norm(0, 0)
            second_norm(0, 1)
            second_norm(0, 2)
            odd_low(0, 1)
            add_attention(10)
            second_norm(0, 3)
            add_attention(11)
            odd_low(0, 3)
            add_square(11)
            second_norm(0, 4)
            split_slot(split_l, 2, 2, 32, fl_ready, wl)
            second_norm(0, 5)
            odd_low(0, 5)
            second_mean(1)
            second_norm(0, 6)
            second_root(1)
            second_norm(0, 7)
            odd_low(0, 7)
            for t in range(0, KT, 2):
                second_norm(1, t)
                if t:
                    odd_low(1, t - 1)
                second_norm(1, t + 1)
            odd_low(1, KT - 1)

            def gate_branch(f, w):
                dve.wait_ge(gate_done, f + 1)
                dve.wait_ge(fstrip_done, 2 * f + 2)
                nc.vector.tensor_tensor(gate[:], gate[:], banks[2 * w + 1][:], ALU.mult).then_inc(gated, 1)
                dve.wait_ge(act_h_done, f + 1)
                nc.vector.tensor_tensor(tile_of(act_l, f), gate[:], tile_of(act_h, f).bitcast(F32),
                                        ALU.subtract).then_inc(act_l_done, 1)

            def up(i):
                for w in range(2):
                    f = 2 * i + w
                    for u in range(2):
                        split_ffn(split_l, i, 2 * w + u, fl_ready, wl)
                        if u == 0 and not (isinstance(f, int) and f == 0):
                            gate_branch(f - 1, 1 - w)
                        if u == 1:
                            for back, done, before in ((1, tap1_done, tap2_done), (2, tap0_done, tap1_done)):
                                dve.wait_ge(before, f + 1)
                                nc.vector.scalar_tensor_tensor(gate_in[:, back:T], banks[2 * w][:, 0:T - back],
                                                               tap(2 - back, f), gate_in[:, back:T],
                                                               ALU.mult, ALU.add).then_inc(done, 1)
            up(0)
            with dve.Fori(1, FT // 2) as i:
                up(i)
            gate_branch(FT - 1, 1)

            def down(k, u, pair):
                if not (isinstance(k, int) and k >= FT - 3):
                    split_down(split_l, k, u, pair, fl_ready, wl)
            downs(dve, down)

            def add_ffn(o, tokens=slice(0, T)):
                dve.wait_ge(y_done, o + 1)
                nc.vector.scalar_tensor_tensor(xT[:, o, tokens], y_bank(o)[:, tokens], mod[:, 5 * KT + o:5 * KT + o + 1],
                                               xT[:, o, tokens], ALU.mult, ALU.add).then_inc(x2_done, 1)

            def last_root(pair):
                lo = 2 * NT + 2 * pair
                at = slice(2 * pair, 2 * pair + 2)
                dve.wait_ge(ssq_done, NT + 2 * (pair + 1))
                nc.vector.tensor_tensor(root[:, 0, lo:lo + 2], ssq_o[:, at, 0], ssq_o[:, at, 1], ALU.add).then_inc(rstd_step, 1)
                dve.wait_ge(rstd_step, 3 * pair + 1)
                nc.vector.tensor_scalar(root[:, 1, lo:lo + 2], root[:, 0, lo:lo + 2], 1.0 / D, EPS, ALU.mult, ALU.add
                                        ).then_inc(rstd_step, 1)
                dve.wait_ge(root_o_done, pair + 1)
                nc.vector.reciprocal(root[:, ROOT_STEPS, lo:lo + 2], root[:, 2, lo:lo + 2]).then_inc(rstd_step, 1)
                dve.wait_ge(rstd_step, 3 * pair + 3)

            def add_gain(m):
                dve.wait_ge(ssq_done, m + 1)
                nc.vector.tensor_tensor(out_part(out_n, m), y_bank(m)[:], nfin[:, T * (m // 4):T * (m // 4 + 1)], ALU.mult
                                        ).then_inc(gained, 1)

            def output(m):
                nc.vector.scalar_tensor_tensor(out_part(out_n, m), y_bank(m)[:],
                                               root[:, ROOT_STEPS, 2 * NT + m % 4:2 * NT + m % 4 + 1],
                                               nfin[:, T * (m // 4):T * (m // 4 + 1)], ALU.mult, ALU.mult
                                               ).then_inc(out_done, 1)

            for o in range(5):
                add_ffn(o)
            dve.wait_ge(nfin_in, 16)
            add_ffn(5)
            add_gain(0)
            add_ffn(6)
            add_gain(1)
            add_ffn(7, slice(0, HALF))
            add_ffn(7, slice(HALF, T))
            add_gain(2)
            add_gain(3)
            last_root(0)
            output(4)
            output(5)
            last_root(1)
            output(6)
            output(7)


_INS = ["x", "c", "w_ada", "b_ada", "norm_mix", "norm_ffn", "attn_w_in", "attn_w_out",
        "ffn_w_up", "ffn_conv_w", "ffn_conv_b", "ffn_w_down", "norm_final"]


def kernel(**inputs):
    import numpy as np
    import concourse.bacc as bacc
    from concourse.bass_utils import run_bass_kernel_spmd

    nc = bacc.Bacc("TRN2", target_bir_lowering=False, num_devices=1)
    arrays, args = {}, []
    for name in _INS:
        a = np.ascontiguousarray(inputs[name])
        arrays[f"in_{name}"] = a
        args.append(nc.dram_tensor(f"in_{name}", a.shape, mybir.dt.from_np(a.dtype), kind="ExternalInput").ap())
    shape = (1, T, D)
    args.append(nc.dram_tensor("out_x", shape, F32, kind="ExternalOutput").ap())
    decoder_layer(nc, *args)
    r = run_bass_kernel_spmd(nc, [arrays], core_ids=[0])
    return r.results[0]["out_x"]
```
